# Optimizing a Trainium2 kernel written in Bass

```python
import jax
import jax.numpy as jnp
from jax import lax
import numpy as np

D_MODEL = 1024
BATCH = 1
SEQ = 256
DEPTH = 2

CTX_LEN = 256
GRID_W = 64
ML_HEADS = 4
ML_DQK = 64
ML_DV = 128
ML_CHUNK = 64
MLA_HEADS = 8
MLA_Q_RANK = 384
MLA_KV_RANK = 256
MLA_NOPE = 64
MLA_ROPE = 32
MLA_V = 64
NA_HEADS = 8
NA_DH = 64
NA_WIN_R = 8
NA_WIN_C = 16
D_FF = 4 * D_MODEL
N_BRANCH = 3
ROPE_THETA = 10000.0
Q_BLOCK = 128
EPS = 1e-6
NEG_INF = -1e30
IN_SIZES = (
    ML_HEADS * ML_DQK, ML_HEADS * ML_DQK, ML_HEADS * ML_DV, ML_HEADS * ML_DV, 4 * ML_HEADS,
    MLA_Q_RANK, MLA_KV_RANK, MLA_ROPE,
    NA_HEADS * NA_DH, NA_HEADS * NA_DH, NA_HEADS * NA_DH,
    N_BRANCH * D_MODEL,
)
D_IN = sum(IN_SIZES)

kernel_name = 'hybrid_mlstm_mla_natten_dit'

def rms_norm(x, g):
    xf = x.astype(jnp.float32)
    y = xf * lax.rsqrt(jnp.mean(xf * xf, axis=-1, keepdims=True) + EPS)
    return (y * g.astype(jnp.float32)).astype(x.dtype)

def split_heads(t, n_heads):
    b, s, _ = t.shape
    return t.reshape(b, s, n_heads, -1)

def swap_ht(t):
    return t.transpose(0, 2, 1, 3)

def split_in(p):
    offsets = np.cumsum(IN_SIZES)[:-1].tolist()
    return jnp.split(p, offsets, axis=-1)

def attend(q, k, v, scale):
    s = jnp.einsum('bhqd,bhkd->bhqk', q, k).astype(jnp.float32) * scale
    p = jax.nn.softmax(s, axis=-1).astype(v.dtype)
    return jnp.einsum('bhqk,bhkd->bhqd', p, v)

def attend_blocked(q, k, v, scale):
    b, h, t, d = q.shape
    nb = t // Q_BLOCK
    qb = q.reshape(b, h, nb, Q_BLOCK, d).transpose(2, 0, 1, 3, 4)
    o = lax.map(lambda qi: attend(qi, k, v, scale), qb)
    return o.transpose(1, 2, 0, 3, 4).reshape(b, h, t, v.shape[-1])

def axial_rope_tables(t, dtype):
    nf = MLA_ROPE // 4
    inv = jnp.power(ROPE_THETA, -jnp.arange(nf, dtype=jnp.float32) / nf)
    pos = jnp.arange(t)
    ang_r = (pos // GRID_W).astype(jnp.float32)[:, None] * inv
    ang_c = (pos % GRID_W).astype(jnp.float32)[:, None] * inv
    return tuple(a[None, :, None, :].astype(dtype) for a in (jnp.cos(ang_r), jnp.sin(ang_r), jnp.cos(ang_c), jnp.sin(ang_c)))

def rotate(x, cos, sin):
    x1, x2 = jnp.split(x, 2, axis=-1)
    return jnp.concatenate([x1 * cos - x2 * sin, x2 * cos + x1 * sin], axis=-1)

def axial_rope(x, tabs):
    cos_r, sin_r, cos_c, sin_c = tabs
    half = x.shape[-1] // 2
    return jnp.concatenate([rotate(x[..., :half], cos_r, sin_r), rotate(x[..., half:], cos_c, sin_c)], axis=-1)

def mlstm_chunked(q, k, v, ig, lf, state, want_h):
    b, h, t, dk = q.shape
    nc = t // ML_CHUNK

    def chunks(a):
        return jnp.moveaxis(a.reshape(b, h, nc, ML_CHUNK, *a.shape[3:]), 2, 0)

    xs = tuple(chunks(a) for a in (q * dk ** -0.5, k, v, ig, lf))
    lower = jnp.tril(jnp.ones((ML_CHUNK, ML_CHUNK), dtype=bool))

    def step(carry, inp):
        C, n, m = carry
        qc, kc, vc, ic, fc = inp
        bcum = jnp.cumsum(fc, axis=-1)
        btot = bcum[..., -1]
        w_end = btot[..., None] - bcum + ic
        m_new = jnp.maximum(btot + m, jnp.max(w_end, axis=-1))
        a_state = jnp.exp(btot + m - m_new)
        wk = jnp.exp(w_end - m_new[..., None])
        C_new = a_state[..., None, None] * C + jnp.einsum('bhl,bhld,bhle->bhde', wk, kc, vc)
        n_new = a_state[..., None] * n + jnp.einsum('bhl,bhld->bhd', wk, kc)
        carry_new = (C_new, n_new, m_new)
        if not want_h:
            return carry_new, None
        dmat = jnp.where(lower, bcum[..., :, None] - bcum[..., None, :] + ic[..., None, :], -jnp.inf)
        inter = bcum + m[..., None]
        m_t = jnp.maximum(inter, jnp.max(dmat, axis=-1))
        a_inter = jnp.exp(inter - m_t)
        s = jnp.einsum('bhtd,bhsd->bhts', qc, kc) * jnp.exp(dmat - m_t[..., None])
        num = a_inter[..., None] * jnp.einsum('bhtd,bhde->bhte', qc, C) + jnp.einsum('bhts,bhse->bhte', s, vc)
        den = a_inter * jnp.einsum('bhtd,bhd->bht', qc, n) + jnp.sum(s, axis=-1)
        h_out = num / jnp.maximum(jnp.abs(den), jnp.exp(-m_t))[..., None]
        return carry_new, h_out

    state, hs = lax.scan(step, state, xs)
    if not want_h:
        return None, state
    return jnp.moveaxis(hs, 0, 2).reshape(b, h, t, -1), state

def mlstm_branch(lat, ctx, i_bias, f_bias, g_out, w_o, want_ctx):
    f32 = jnp.float32

    def prep(q, k, v, gates):
        b, t, _ = q.shape
        qh, kh, vh = (swap_ht(split_heads(a, ML_HEADS)).astype(f32) for a in (q, k, v))
        g = gates.astype(f32).reshape(b, t, 4, ML_HEADS).transpose(2, 0, 3, 1)
        dirs = [(g[2 * d] + i_bias[d].astype(f32)[None, :, None],
                 jax.nn.log_sigmoid(g[2 * d + 1] + f_bias[d].astype(f32)[None, :, None])) for d in range(2)]
        return qh, kh, vh, dirs

    ql, kl, vl, dl = prep(lat[0], lat[1], lat[2], lat[4])
    qc, kc, vc, dc = prep(ctx[0], ctx[1], ctx[2], ctx[4])
    b = qc.shape[0]
    zero = (jnp.zeros((b, ML_HEADS, ML_DQK, ML_DV), f32), jnp.zeros((b, ML_HEADS, ML_DQK), f32), jnp.zeros((b, ML_HEADS), f32))
    h_lat, h_ctx = [], []
    for d in range(2):
        flip = (lambda a: jnp.flip(a, axis=2)) if d == 1 else (lambda a: a)
        hc_d, st = mlstm_chunked(flip(qc), flip(kc), flip(vc), flip(dc[d][0]), flip(dc[d][1]), zero, want_ctx)
        hl_d, _ = mlstm_chunked(flip(ql), flip(kl), flip(vl), flip(dl[d][0]), flip(dl[d][1]), st, True)
        h_lat.append(flip(hl_d))
        if want_ctx:
            h_ctx.append(flip(hc_d))

    def out(hsum, o):
        bb, _, t, _ = hsum.shape
        hn = rms_norm(swap_ht(hsum), g_out.reshape(ML_HEADS, ML_DV)).reshape(bb, t, -1).astype(o.dtype)
        return (hn * jax.nn.sigmoid(o)) @ w_o

    y = out(h_lat[0] + h_lat[1], lat[3])
    yc = out(h_ctx[0] + h_ctx[1], ctx[3]) if want_ctx else None
    return y, yc

def mla_branch(lat, ctx, g_cq, w_uq, g_ckv, w_ukv, g_q, g_k, w_o, rope, want_ctx):
    scale = (MLA_NOPE + MLA_ROPE) ** -0.5

    def qkv(dq, dkv, kr, rope_tabs, need_q):
        b, t, _ = dkv.shape
        kv = (rms_norm(dkv, g_ckv) @ w_ukv).reshape(b, t, MLA_HEADS, MLA_NOPE + MLA_V)
        k_r = jnp.broadcast_to(kr[:, :, None, :], (b, t, MLA_HEADS, MLA_ROPE))
        k = rms_norm(jnp.concatenate([kv[..., :MLA_NOPE], k_r], axis=-1), g_k)
        q = None
        if need_q:
            q = rms_norm((rms_norm(dq, g_cq) @ w_uq).reshape(b, t, MLA_HEADS, MLA_NOPE + MLA_ROPE), g_q)
        if rope_tabs is not None:
            k = jnp.concatenate([k[..., :MLA_NOPE], axial_rope(k[..., MLA_NOPE:], rope_tabs)], axis=-1)
            q = jnp.concatenate([q[..., :MLA_NOPE], axial_rope(q[..., MLA_NOPE:], rope_tabs)], axis=-1)
        return (swap_ht(q) if need_q else None), swap_ht(k), swap_ht(kv[..., MLA_NOPE:])

    ql, kl, vl = qkv(*lat, rope, True)
    qc, kc, vc = qkv(*ctx, None, want_ctx)
    k_all = jnp.concatenate([kc, kl], axis=2)
    v_all = jnp.concatenate([vc, vl], axis=2)
    o = attend_blocked(ql, k_all, v_all, scale)
    b, _, t, _ = o.shape
    y = swap_ht(o).reshape(b, t, -1) @ w_o
    yc = None
    if want_ctx:
        oc = attend(qc, kc, vc, scale)
        yc = swap_ht(oc).reshape(b, oc.shape[2], -1) @ w_o
    return y, yc

def natten_branch(lat, ctx, g_q, g_k, rpb, w_o, want_ctx):
    scale = NA_DH ** -0.5
    f32 = jnp.float32

    def heads(q, k, v):
        q, k, v = (split_heads(a, NA_HEADS) for a in (q, k, v))
        return swap_ht(rms_norm(q, g_q)), swap_ht(rms_norm(k, g_k)), swap_ht(v)

    ql, kl, vl = heads(*lat)
    qc, kc, vc = heads(*ctx)
    b, h, t, dh = ql.shape
    rows = t // GRID_W
    wr = min(NA_WIN_R, rows)
    n_band = wr * GRID_W
    kg = kl.reshape(b, h, rows, GRID_W, dh)
    vg = vl.reshape(b, h, rows, GRID_W, dh)
    col = jnp.arange(GRID_W)
    cs = jnp.clip(col - NA_WIN_C // 2, 0, GRID_W - NA_WIN_C)
    col_ok = (col[None, :] >= cs[:, None]) & (col[None, :] < cs[:, None] + NA_WIN_C)
    dc_idx = jnp.clip(col[None, :] - col[:, None] + NA_WIN_C - 1, 0, 2 * NA_WIN_C - 2)

    def one_row(args):
        r, q_row = args
        rs = jnp.clip(r - wr // 2, 0, rows - wr)
        k_band = lax.dynamic_slice_in_dim(kg, rs, wr, axis=2)
        v_band = lax.dynamic_slice_in_dim(vg, rs, wr, axis=2)
        dr_idx = rs + jnp.arange(wr) - r + NA_WIN_R - 1
        bias = rpb[:, dr_idx[None, :, None], dc_idx[:, None, :]].astype(f32)
        s_win = jnp.einsum('bhqd,bhrkd->bhqrk', q_row, k_band).astype(f32) * scale + bias
        s_win = jnp.where(col_ok[:, None, :], s_win, NEG_INF)
        s_ctx = jnp.einsum('bhqd,bhcd->bhqc', q_row, kc).astype(f32) * scale
        p = jax.nn.softmax(jnp.concatenate([s_win.reshape(b, h, GRID_W, n_band), s_ctx], axis=-1), axis=-1).astype(vl.dtype)
        return (jnp.einsum('bhqn,bhnd->bhqd', p[..., :n_band], v_band.reshape(b, h, n_band, dh))
                + jnp.einsum('bhqc,bhcd->bhqd', p[..., n_band:], vc))

    o = lax.map(one_row, (jnp.arange(rows), jnp.moveaxis(ql.reshape(b, h, rows, GRID_W, dh), 2, 0)))
    y = o.transpose(1, 0, 3, 2, 4).reshape(b, t, h * dh) @ w_o
    yc = None
    if want_ctx:
        oc = attend(qc, kc, vc, scale)
        yc = swap_ht(oc).reshape(b, oc.shape[2], -1) @ w_o
    return y, yc

def merge(y_a, y_b, y_c, gate_pre, w_out):
    g = jax.nn.sigmoid(gate_pre.astype(jnp.float32)).astype(y_a.dtype)
    g_a, g_b, g_c = jnp.split(g, N_BRANCH, axis=-1)
    return (g_a * y_a + g_b * y_b + g_c * y_c) @ w_out

def token_mixer(h, hc, rope, want_ctx, w_in, ml_i_bias, ml_f_bias, ml_g_out, ml_w_o,
                mla_g_cq, mla_w_uq, mla_g_ckv, mla_w_ukv, mla_g_q, mla_g_k, mla_w_o,
                na_g_q, na_g_k, na_rpb, na_w_o, w_out):
    p = split_in(h @ w_in)
    pc = split_in(hc @ w_in)
    y_a, yc_a = mlstm_branch(p[0:5], pc[0:5], ml_i_bias, ml_f_bias, ml_g_out, ml_w_o, want_ctx)
    y_b, yc_b = mla_branch(p[5:8], pc[5:8], mla_g_cq, mla_w_uq, mla_g_ckv, mla_w_ukv, mla_g_q, mla_g_k, mla_w_o, rope, want_ctx)
    y_c, yc_c = natten_branch(p[8:11], pc[8:11], na_g_q, na_g_k, na_rpb, na_w_o, want_ctx)
    y = merge(y_a, y_b, y_c, p[11], w_out)
    yc = merge(yc_a, yc_b, yc_c, pc[11], w_out) if want_ctx else None
    return y, yc

def sqrelu_mlp(h, w1, w2):
    return jnp.square(jax.nn.relu(h @ w1)) @ w2

def setup_inputs(seed: int = 0) -> dict:
    key = jax.random.key(seed)
    ks = iter(jax.random.split(key, 32))

    def nrm(shape, s):
        return jax.random.normal(next(ks), shape, jnp.float32) * s

    L, D = DEPTH, D_MODEL
    return {
        'x': nrm((BATCH, SEQ, D), 1.0),
        'c': nrm((BATCH, D), 1.0),
        'ctx': nrm((BATCH, CTX_LEN, D), 1.0),
        'c_ctx': nrm((D,), 1.0),
        'w_mod': nrm((L, D, 6 * D), 0.3 * D ** -0.5),
        'b_mod': nrm((L, 6 * D), 0.02),
        'g_norm1': 1.0 + nrm((L, D), 0.05),
        'g_norm2': 1.0 + nrm((L, D), 0.05),
        'w_in': nrm((L, D, D_IN), D ** -0.5),
        'ml_i_bias': nrm((L, 2, ML_HEADS), 0.1),
        'ml_f_bias': 3.0 + nrm((L, 2, ML_HEADS), 0.5),
        'ml_g_out': 1.0 + nrm((L, ML_HEADS * ML_DV), 0.05),
        'ml_w_o': nrm((L, ML_HEADS * ML_DV, D), (ML_HEADS * ML_DV) ** -0.5),
        'mla_g_cq': 1.0 + nrm((L, MLA_Q_RANK), 0.05),
        'mla_w_uq': nrm((L, MLA_Q_RANK, MLA_HEADS * (MLA_NOPE + MLA_ROPE)), MLA_Q_RANK ** -0.5),
        'mla_g_ckv': 1.0 + nrm((L, MLA_KV_RANK), 0.05),
        'mla_w_ukv': nrm((L, MLA_KV_RANK, MLA_HEADS * (MLA_NOPE + MLA_V)), MLA_KV_RANK ** -0.5),
        'mla_g_q': 1.0 + nrm((L, MLA_NOPE + MLA_ROPE), 0.05),
        'mla_g_k': 1.0 + nrm((L, MLA_NOPE + MLA_ROPE), 0.05),
        'mla_w_o': nrm((L, MLA_HEADS * MLA_V, D), (MLA_HEADS * MLA_V) ** -0.5),
        'na_g_q': 1.0 + nrm((L, NA_DH), 0.05),
        'na_g_k': 1.0 + nrm((L, NA_DH), 0.05),
        'na_rpb': nrm((L, NA_HEADS, 2 * NA_WIN_R - 1, 2 * NA_WIN_C - 1), 0.5),
        'na_w_o': nrm((L, NA_HEADS * NA_DH, D), (NA_HEADS * NA_DH) ** -0.5),
        'w_out': nrm((L, D, D), D ** -0.5),
        'w_ff1': nrm((L, D, D_FF), D ** -0.5),
        'w_ff2': nrm((L, D_FF, D), D_FF ** -0.5),
    }

def reference(x, c, ctx, c_ctx, w_mod, b_mod, g_norm1, g_norm2, w_in, ml_i_bias, ml_f_bias, ml_g_out, ml_w_o,
              mla_g_cq, mla_w_uq, mla_g_ckv, mla_w_ukv, mla_g_q, mla_g_k, mla_w_o,
              na_g_q, na_g_k, na_rpb, na_w_o, w_out, w_ff1, w_ff2):
    rope = axial_rope_tables(x.shape[1], x.dtype)
    xc = ctx
    for l in range(DEPTH):
        want_ctx = l < DEPTH - 1
        mod = jax.nn.silu(c) @ w_mod[l] + b_mod[l]
        sh1, sc1, g1, sh2, sc2, g2 = jnp.split(mod[:, None, :], 6, axis=-1)
        modc = jax.nn.silu(c_ctx) @ w_mod[l] + b_mod[l]
        shc1, scc1, gc1, shc2, scc2, gc2 = jnp.split(modc, 6, axis=-1)
        h = rms_norm(x, g_norm1[l]) * (1 + sc1) + sh1
        hc = rms_norm(xc, g_norm1[l]) * (1 + scc1) + shc1
        y, yc = token_mixer(h, hc, rope, want_ctx, w_in[l], ml_i_bias[l], ml_f_bias[l], ml_g_out[l], ml_w_o[l],
                            mla_g_cq[l], mla_w_uq[l], mla_g_ckv[l], mla_w_ukv[l], mla_g_q[l], mla_g_k[l], mla_w_o[l],
                            na_g_q[l], na_g_k[l], na_rpb[l], na_w_o[l], w_out[l])
        x = x + g1 * y
        x = x + g2 * sqrelu_mlp(rms_norm(x, g_norm2[l]) * (1 + sc2) + sh2, w_ff1[l], w_ff2[l])
        if want_ctx:
            xc = xc + gc1 * yc
            xc = xc + gc2 * sqrelu_mlp(rms_norm(xc, g_norm2[l]) * (1 + scc2) + shc2, w_ff1[l], w_ff2[l])
    return x


_drawn_inputs = setup_inputs


def setup_inputs(seed=0):
    import zlib

    import numpy as np

    out = dict(_drawn_inputs(seed))
    spreads = {}
    factors = {'g_norm1': 5.474,
     'g_norm2': 2.931,
     'ml_i_bias': 29.171,
     'ml_f_bias': 2.704,
     'ml_g_out': 8.0,
     'mla_g_cq': 8.0,
     'mla_w_uq': 4.888,
     'mla_g_ckv': 8.0,
     'mla_g_q': 8.0,
     'mla_g_k': 8.0,
     'na_g_q': 8.0,
     'na_g_k': 8.0,
     'na_rpb': 8.0}
    for name, (base, spread) in spreads.items():
        noise = np.random.default_rng([zlib.crc32(name.encode()), seed]).standard_normal(out[name].shape)
        drawn = base * np.exp(spread * noise) if base else spread * noise
        out[name] = jnp.asarray(drawn.astype(out[name].dtype))
    for name, factor in factors.items():
        out[name] = (out[name] * factor).astype(out[name].dtype)
    return out
```

```python
from contextlib import ExitStack

import numpy as np
import concourse.bass as bass
import concourse.mybir as mybir

F32 = mybir.dt.float32
F32R = mybir.dt.float32r
ALU = mybir.AluOpType
ACT = mybir.ActivationFunctionType
AX = mybir.AxisListType.X

D = 1024
SEQ = 256
CTX = 256
TOK = SEQ + CTX
DEPTH = 2
GRID_W = 64
GRID_H = SEQ // GRID_W
P = 128
KC = D // P
DFF = 4 * D
NTILE = TOK // P
BLK = 256
EPS = 1e-6
ML_H, ML_DK, ML_DV = 4, 64, 128
HEADS = 8
MLA_QR, MLA_KVR, NOPE, ROPE, MLA_V = 384, 256, 64, 32, 64
MLA_D = NOPE + ROPE
NA_D = 64
WIN_R, WIN_C = 8, 16
RPB_R, RPB_C = 2 * WIN_R - 1, 2 * WIN_C - 1
NEG = -1e30
SIZES = (256, 256, 512, 512, 16, MLA_QR, MLA_KVR, ROPE, 512, 512, 512, 3 * D)
OFF = [sum(SIZES[:i]) for i in range(len(SIZES))]
(O_MLQ, O_MLK, O_MLV, O_MLO, O_GATE, O_DQ, O_DKV, O_KR, O_NAQ, O_NAK, O_NAV, O_MERGE) = OFF
MLA_SCALE = MLA_D ** -0.5
NA_SCALE = NA_D ** -0.5

R_G1, R_G2, R_BMOD, R_GOUT, R_GCQ, R_GCKV, R_GQ, R_GK, R_NGQ, R_NGK, R_C, R_CC = (
    0, 8, 16, 64, 68, 71, 73, 74, 75, 76, 77, 85)
N_ROWS = 96
M_SH1, M_SC1, M_GATE1, M_SH2, M_SC2, M_GATE2 = (8 * i for i in range(6))
LAT, CTXS = 0, 1

C_ID, C_ONE, C_SEL, C_MASK, C_COS, C_SIN, C_FLIP = 0, 128, 256, 768, 832, 896, 960
N_CONST = 1088


def shape_constants():
    c = np.zeros((P, N_CONST), np.float32)
    c[:, C_ID:C_ID + P] = np.eye(P)
    c[:, C_ONE:C_ONE + P] = 1.0
    for h in range(ML_H):
        c[h, C_SEL + P * h:C_SEL + P * h + P] = 1.0
    col = np.arange(GRID_W)
    start = np.clip(col - WIN_C // 2, 0, GRID_W - WIN_C)
    ok = (col[None, :] >= start[:, None]) & (col[None, :] < start[:, None] + WIN_C)
    c[:, C_MASK:C_MASK + GRID_W] = np.tile(np.where(ok, 0.0, NEG)[::-1], (2, 1))
    for g in range(2):
        for r in range(GRID_W):
            c[GRID_W * g + r, C_FLIP + GRID_W * g + GRID_W - 1 - r] = 1.0
    nf = ROPE // 4
    inv = np.power(np.float32(10000.0), -np.arange(nf, dtype=np.float32) / np.float32(nf)).astype(np.float32)
    pos = np.arange(SEQ)
    for part, at in enumerate((pos // GRID_W, pos % GRID_W)):
        ang = at.astype(np.float32)[:, None] * inv
        for tile in range(SEQ // P):
            rows = slice(tile * P, tile * P + P)
            base = tile * ROPE + part * 2 * nf
            c[:, C_COS + base:C_COS + base + nf] = np.cos(ang[rows])
            c[:, C_COS + base + nf:C_COS + base + 2 * nf] = np.cos(ang[rows])
            c[:, C_SIN + base:C_SIN + base + nf] = -np.sin(ang[rows])
            c[:, C_SIN + base + nf:C_SIN + base + 2 * nf] = np.sin(ang[rows])
    return c


class Sem:

    def __init__(self, handle, base=0):
        self.handle, self.base, self.n = handle, base, 0

    def up(self, by):
        self.n += by
        return self.handle

    def at(self, value):
        return self.handle, self.base + value


class Steps:

    def __init__(self, eng, sem):
        self.eng, self.sem, self.n, self.off = eng, sem, 0, 0

    def link(self, instruction):
        instruction.then_inc(self.sem, 1)
        self.n += 1
        self.eng.wait_ge(self.sem, self.off + self.n)

    def enter(self, i, per_turn):
        self.start, self.per_turn, self.off = self.n, per_turn, i * per_turn

    def leave(self, turns):
        assert self.n - self.start == self.per_turn, (self.n - self.start, self.per_turn)
        self.n, self.off = self.start + turns * self.per_turn, 0


MOD_BLOCKS = 6 * D // BLK
SIDE = {("start", 0): 8, ("na", 0): 16, ("mla", 0): 16, ("na", 1): 4, ("mla", 1): 4}
SIDE_AT = {k: sum(list(SIDE.values())[:i]) for i, k in enumerate(SIDE)}


def phases():
    at, n, u = {}, 0, 0

    def add(name, layer, blocks, units):
        nonlocal n, u
        at[name, layer] = (n, u)
        n, u = n + blocks, u + units
    add("start", 0, 8, 0)
    for l in range(DEPTH):
        add("ml", l, 7, 7)
        add("na", l, 6 + SIDE["na", l], 6)
        add("mla", l, 6 + SIDE["mla", l], 11 if l == 0 else 9)
        add("merge", l, 4 * 6, 4 * 6)
        add("wout", l, 4, 4)
        add("ff", l, 4 * 8, 4 * 8)
    at["end", 0] = (n, u)
    return at


AT = phases()
N_BLOCKS = AT["end", 0][0]


def first_token(l):
    return 0 if l < DEPTH - 1 else CTX


def mla_units(l):
    return [1, 1, 1] + ([2, 2] if l == 0 else [1, 1]) + [4]


def ml_pieces(d, t0):
    lat = [(0, 0, 256, 512, None), (1, 1, 256, 512, None)]
    if d == 0:
        lat += [(2, 2, 256, 512, 2), (3, 3, 384, 512, 3)]
        con = [(4, 0, 0, 256, 0), (5, 1, 128, 256, 1)]
    else:
        lat += [(2, 2, 256, 384, 2), (3, 3, 256, 512, 3)]
        con = [(5, 1, 0, 256, 1), (4, 0, 0, 128, 0)]
    return lat + (con if t0 == 0 else [])


def att_tiles(l):
    return range(first_token(l) // P, NTILE)


def att_keys(t):
    return 2 if t < 2 else 4


def norm_banks(br, l):
    if br == "na":
        for j in range(2):
            for b in range(2):
                yield (True, 2 * b, 2, 4 * j, 4) if l == 0 else (True, 2 + b, 1, 4 * j, 4)
        for j in range(2):
            for b in range(2):
                yield (False, 2 * b, 2, 4 * j, 4)
    else:
        for j in range(2):
            for t in att_tiles(l):
                yield (True, t, 1, 4 * j, 4)
        for t in range(NTILE):
            for j in range(2):
                yield (False, t, 1, 4 * j, 4)


def signals(phase, l):
    if phase == "nrm":
        halves = 1 if l == 3 else 2
        return dict(sq=KC, sum=KC, std=1, t=KC, t2=KC, high=KC * halves, low=KC)
    if phase == "mg":
        return dict(acc=1, high=KC, low=KC)
    if phase == "ff":
        return dict(high=32, hid=32)
    if phase == "ml":
        pieces = len(ml_pieces(0, first_token(l)))
        diag = sum(p[4] is not None for p in ml_pieces(0, first_token(l)))
        hd = 2 * ML_H
        return dict(zero=2, exp=hd * pieces, mask=hd * diag, arg=hd * pieces, sc=ML_H, P=hd * pieces, nm=hd, dm=hd, rc=hd, en=hd,
                    bcM=hd, nd=hd, acc=hd, h=ML_H, sq=ML_H, ssum=ML_H, std=ML_H, y=ML_H, oH=ML_H, nz=2, ln=2,
                    nmrow=2, gT=1, gcol=1, turned=1, small=1, rows=4)
    nb = list(norm_banks(phase, l))
    nq = sum(q for q, *_ in nb)
    tiles = len(att_tiles(l))
    n = dict(g=1, tr=len(nb), trq=nq, trk=len(nb) - nq, nsq=len(nb), ss=len(nb), nstd=len(nb))
    n |= {k: tiles * HEADS for k in ("s", "p", "pt", "pts", "o", "oev", "max")}
    n |= dict(ot=tiles, oH=tiles, oL=tiles)
    if phase == "na":
        return n | dict(zero=1, rpb=12 * 16)
    return n | dict(csq=5, csum=5, cstd=2, cn=5, cH=5, cL=5, krs=4, krsum=4, st=len(nb))


def build(nc, a, out):
    ctx = ExitStack()
    with ctx:
        def sb(name, shape, dt=F32):
            return ctx.enter_context(nc.sbuf_tensor(name, shape, dt))

        sems, handles = {}, {}

        def S(name):
            if name not in sems:
                phase, _, what = name.partition("_")
                base, hw = 0, name
                if what and phase[-1].isdigit():
                    kind = phase.rstrip("0123456789")
                    turn = 2 * int(phase[3]) + int(phase[4]) if kind == "nrm" else int(phase[-1])
                    hw = f"{kind}_{what}"
                    base = sum(signals(kind, t)[what] for t in range(turn))
                if hw not in handles:
                    handles[hw] = ctx.enter_context(nc.semaphore(hw))
                sems[name] = Sem(handles[hw], base)
            return sems[name]

        raw = sb("raw", [P, 2, 2048])
        wH = sb("wH", [P, 2, 2048], F32R)
        wL = sb("wL", [P, 2, 2048], F32R)
        hH = sb("hH", [P, KC, TOK], F32R)
        hL = sb("hL", [P, KC, TOK], F32R)
        oH = sb("oH", [P, 13, TOK], F32R)
        oL = sb("oL", [P, 13, TOK], F32R)
        arena = sb("arena", [P, 15872])
        const = sb("const", [P, N_CONST])
        par = sb("par", [P, DEPTH, N_ROWS])
        modT = sb("modT", [P, DEPTH, 48, 2])
        modt = sb("modt", [32, BLK])
        gain = sb("gain", [P, KC, 2])
        ccols = sb("ccols", [P, KC, P], F32R)
        csilu = sb("csilu", [P, 2, KC])
        small = sb("small", [P, NTILE, 64])
        ropeg = sb("ropeg", [P, DEPTH, 2, ROPE])
        bias4 = sb("bias4", [4, DEPTH, 2, 2])
        gcols = sb("gcols", [P, 2])
        stat = sb("stat", [P, 192])
        eps = sb("eps", [P, 1])

        def view(at, *dims):
            n = int(np.prod(dims))
            v = arena[:, at:at + n]
            if len(dims) == 2:
                return v.rearrange("p (a b) -> p a b", a=dims[0])
            if len(dims) == 3:
                return v.rearrange("p (a b c) -> p a b c", a=dims[0], b=dims[1])
            return v

        x = view(0, KC, TOK)
        ident = const[:, C_ID:C_ID + P]
        flip = const[:, C_FLIP:C_FLIP + P]
        ones = const[:, C_ONE:C_ONE + P]
        bank = [ctx.enter_context(nc.psum_tensor(f"bank{b}", [P, 512], F32)) for b in range(8)]
        prow = view(12288, DEPTH, P)[0:N_ROWS]
        x_spill = nc.dram_tensor("x_spill", (P, KC * TOK), F32).ap()

        n_sq, n_std, n_t, n_t2 = view(4096, 2, TOK), view(5120, TOK), view(5632, 2, TOK), view(6656, 2, TOK)
        xtok = view(8192, NTILE, D)
        m_qz, m_k, m_v, m_o = view(0, 4, TOK), view(2048, 2, TOK), view(3072, 4, 512), view(5120, 4, TOK)
        m_rows = view(7168, 4, TOK)
        m_z, m_e, m_F = view(9728, TOK), view(10240, TOK), view(10752, TOK)
        m_g = view(11264, 2, TOK)
        m_E = (view(12288, 6, 256), view(10240, 6, 256))
        m_en, m_d, m_tmp = view(13824, TOK), view(14336, TOK), view(14848, TOK)
        m_h = (view(15360, TOK), view(9216, TOK))
        m_sq = m_z
        gcol = stat[:, 128:160]
        a_q, a_k, a_v, a_tb = view(0, 8, TOK), view(4096, 4, TOK), view(6144, 4, 512), view(8192, 8, 6, 64)
        l_q, l_k, l_v = view(0, 8, TOK), view(4096, 8, TOK), view(8192, 4, 512)
        l_c = view(12800, 5, TOK)
        l_kr = view(10240, 4, ROPE)
        l_r = view(10368, 2, 128)
        st, s_sq, s_sq2 = view(11264, 2, 512), view(12288, 512), view(15360, 512)
        s_p, s_pt, s_o = view(12800, 2, 512), view(13824, 2, 512), view(14848, 2, 512)
        l_t = view(10624, ROPE)
        g_acc, g_sig, g_tmp = view(4096, KC, TOK), view(8192, 2, TOK), view(9216, 2, TOK)
        f_r, f_h = view(4096, 2, TOK), view(5120, 2, TOK)

        w_in = [a["w_in"][l].rearrange("(k p) m -> p k m", p=P) for l in range(DEPTH)]
        w_mod = [a["w_mod"][l].rearrange("(k p) m -> p k m", p=P) for l in range(DEPTH)]
        w_ff1 = [a["w_ff1"][l].rearrange("(k p) m -> p k m", p=P) for l in range(DEPTH)]
        w_ff2 = [a["w_ff2"][l].rearrange("(k p) m -> p k m", p=P) for l in range(DEPTH)]
        w_outp = [a["w_out"][l].rearrange("(k p) m -> p k m", p=P) for l in range(DEPTH)]
        w_br = [[a[w][l].rearrange("(k p) m -> p k m", p=P) for w in ("ml_w_o", "mla_w_o", "na_w_o")]
                for l in range(DEPTH)]
        w_uq = [a["mla_w_uq"][l].rearrange("(k p) m -> p k m", p=P) for l in range(DEPTH)]
        w_ukv = [a["mla_w_ukv"][l].rearrange("(k p) m -> p k m", p=P) for l in range(DEPTH)]

        def slot(t, n, k, w):
            return t[:, n % 2, 0:k * w].rearrange("p (k w) -> p k w", k=k)

        def cols(w, c, width=BLK):
            return w[:, :, bass.ds(c, width)]

        def phase_blocks(name, l):
            w = w_in[l]
            if name == "ml":
                yield from ((cols(w, c), KC, BLK) for c in range(0, O_GATE, BLK))
                yield (cols(w, O_GATE, ROPE), cols(w, O_KR, ROPE)), KC, 64
            if name == "na":
                yield from ((cols(w, O_NAQ + c), KC, BLK) for c in range(0, 1536, BLK))
            if name == "mla":
                yield cols(w, O_DQ), KC, BLK
                yield cols(w, O_DQ + BLK), KC, BLK
                yield cols(w, O_DQ + 2 * BLK, P), KC, P
                yield from ((cols(w_uq[l], c, 384), 3, 384) for c in (0, 384))
                yield cols(w_ukv[l], 0, 1024), 2, 1024
            for g in range(SIDE_AT.get((name, l), 0), SIDE_AT.get((name, l), 0) + SIDE.get((name, l), 0)):
                yield cols(w_mod[g // MOD_BLOCKS], g % MOD_BLOCKS * BLK), KC, BLK
            if name == "wout":
                yield from ((cols(w_outp[l], c), KC, BLK) for c in range(0, D, BLK))

        def merge_body(l, i):
            for br in range(3):
                yield "gate", cols(w_in[l], i * BLK + (O_MERGE + br * D)), KC
                yield "branch", cols(w_br[l][br], (i * P) * 2), 4

        def ff_body(l, i):
            for j in range(4):
                yield "up", cols(w_ff1[l], i * D + j * BLK), KC
            for j in range(4):
                yield "down", w_ff2[l][:, bass.ds(i * KC, KC), j * BLK:j * BLK + BLK], KC

        def loops(l):
            return (("merge", merge_body, 6), ("ff", ff_body, 8))

        def side_step(br, l, step):
            every = len(att_tiles(l)) * HEADS // SIDE[br, l]
            k = step // every
            return k if step % every == 0 and k < SIDE[br, l] else None

        SHARED = np.zeros(N_BLOCKS, bool)
        SHARED[0:SIDE["start", 0]] = True
        for l in range(DEPTH):
            SHARED[AT["ml", l][0]:AT["ml", l][0] + 2] = True
            SHARED[AT["merge", l][0]:AT["ff", l][0] + 4 * 8] = True

        def cut_chunk(k):
            return (5 * k + 4) // 8

        def share_step(n):
            k = n + 1
            while k < N_BLOCKS and not SHARED[k]:
                k += 1
            return k - n

        def count(k, i, body):
            return k if i is None else i * body + k

        def half(k, i, body):
            return k // 2 if i is None else i * (body // 2) + k // 2

        block = ctx.enter_context(nc.Block())

        @block.sync
        def _(sp):
            def load(n, src, k, w, i=None, body=0):
                if not (i is None and n < 2):
                    before = count(n - 1, i, body)
                    sp.wait_ge(*S("w_split").at(before))
                    if i is not None or SHARED[n - 2]:
                        sp.wait_ge(*S("w_share").at(before))
                dst = slot(raw, n, k, w)
                if type(src) is tuple:
                    sp.dma_start(dst[:, :, 0:ROPE], src[0]).then_inc(S("raw_gates").handle, 16)
                    dst, src = dst[:, :, ROPE:2 * ROPE], src[1]
                sp.dma_start(dst, src).then_inc(S(f"raw_full{n % 2}").handle, 16)

            start = list(phase_blocks("start", 0))
            for n, (src, k, w) in enumerate(start[:2]):
                load(n, src, k, w)
            for src, dst in ((a["ctx"], 0), (a["x"], 2)):
                sp.dma_start(xtok[:, dst:dst + 2, :], src[0].rearrange("(t p) d -> p t d", p=P)).then_inc(S("x_in").up(16), 16)
            for n, (src, k, w) in enumerate(start[2:], 2):
                load(n, src, k, w)
            for l in range(DEPTH):
                for name in ("ml", "na", "mla"):
                    for j, (src, k, w) in enumerate(phase_blocks(name, l)):
                        load(AT[name, l][0] + j, src, k, w)
                name, make, body = loops(l)[0]
                with sp.Fori(0, 4) as i:
                    for j, (_, src, k) in enumerate(make(l, i)):
                        load(AT[name, l][0] + j, src, k, BLK, i, body)
                for j, (src, k, w) in enumerate(phase_blocks("wout", l)):
                    load(AT["wout", l][0] + j, src, k, w)
                name, make, body = loops(l)[1]
                with sp.Fori(0, 4) as i:
                    for j, (_, src, k) in enumerate(make(l, i)):
                        load(AT[name, l][0] + j, src, k, BLK, i, body)
            sp.wait_ge(*S("y_tok").at(4))
            sp.dma_start(out[0].rearrange("(t p) d -> p t d", p=P), xtok[:, 2:4, :]).then_inc(S("y_out").handle, 16)
            sp.wait_ge(*S("y_out").at(16))

        bar = [0]

        def barrier(eng, k):
            eng.drain().then_inc(S("phase_end").handle, 1)
            eng.wait_ge(S("phase_end").handle, 4 * k)

        @block.gpsimd
        def _(pool):
            phase = [0]

            def end():
                phase[0] += 1
                barrier(pool, phase[0])

            def low(n, k, w, i=None, body=0):
                cut = cut_chunk(k) * w
                if not SHARED[n]:
                    pool.wait_ge(*S("w_high").at(count(2 * n + 1, i, 2 * body)))
                    pool.tensor_tensor(wL[:, n % 2, 0:cut], raw[:, n % 2, 0:cut],
                                       wH[:, n % 2, 0:cut].bitcast(F32), ALU.subtract)
                pool.wait_ge(*S("w_high").at(count(2 * n + 2, i, 2 * body)))
                pool.tensor_tensor(wL[:, n % 2, cut:k * w], raw[:, n % 2, cut:k * w],
                                   wH[:, n % 2, cut:k * w].bitcast(F32), ALU.subtract)\
                    .then_inc(S("w_split").handle, 1)

            sizes = [(KC, BLK)] * SIDE["start", 0]
            for l in range(DEPTH):
                sizes += [(k, w) for name in ("ml", "na", "mla") for _, k, w in phase_blocks(name, l)]
                sizes += [(KC, BLK), (4, BLK)] * (4 * 3) + [(KC, BLK)] * 4 + [(KC, BLK)] * (4 * 8)
            done = [0]

            def low_to(n_end):
                while done[0] < n_end:
                    low(done[0], *sizes[done[0]])
                    done[0] += 1

            def norm_low(l, which, t0):
                tag = f"nrm{l}{which}_"
                for c in range(KC):
                    pool.wait_ge(*S(tag + "t2").at(c + 1))
                    pool.wait_ge(*S(tag + "high").at((2 if t0 == 0 else 1) * (c + 1)))
                    pool.tensor_tensor(hL[:, c, t0:], n_t2[:, c % 2, t0:], hH[:, c, t0:].bitcast(F32),
                                       ALU.subtract).then_inc(S(tag + "low").up(1), 1)

            pool.memset(prow[:, :, :], 0.0).then_inc(S("zeroed").up(1), 1)
            pool.memset(ccols[:, :, :].bitcast(F32), 0.0).then_inc(S("zeroed").up(1), 1)
            pool.memset(eps[:, :], EPS).then_inc(S("zeroed").up(1), 1)
            low_to(8)
            for l in range(DEPTH):
                t0 = first_token(l)
                if l == 0:
                    pool.wait_ge(*S("xT_done").at(8))
                pool.dma_start(x_spill, arena[:, 0:KC * TOK]).then_inc(S("spilled").handle, 16)
                n0 = AT["ml", l][0]
                low_to(n0 + 2)
                norm_low(l, 0, 0)
                pool.wait_ge(*S("spilled").at(16 * (l + 1)))
                pool.wait_ge(*S(f"nrm{l}0_low").at(KC))
                pool.memset(m_rows, 0.0).then_inc(S(f"ml{l}_zero").handle, 1)
                pool.memset(m_qz, 0.0).then_inc(S(f"ml{l}_zero").handle, 1)
                low_to(n0 + 7 + 2)
                k = 0
                for h in range(ML_H):
                    for d in range(2):
                        for e_at, kt, lo, hi, diag in ml_pieces(d, t0):
                            k += 1
                            if diag is None:
                                continue
                            pool.wait_ge(*S(f"ml{l}_exp").at(k))
                            blk_ = m_E[d][:, e_at, diag * P - lo:diag * P - lo + P]
                            sgn = 1 if d == 0 else -1
                            pool.affine_select(out=blk_, in_=blk_, compare_op=ALU.is_ge, fill=0.0, base=0,
                                               pattern=[[sgn, P]], channel_multiplier=-sgn)\
                                .then_inc(S(f"ml{l}_mask").handle, 1)
                end()
                pool.memset(a_q, 0.0).then_inc(S(f"na{l}_zero").handle, 1)
                for j in range(6):
                    for up in range(2):
                        src = bass.AP(a["na_rpb"].tensor,
                                      a["na_rpb"].offset + l * HEADS * RPB_R * RPB_C
                                      + (WIN_R - GRID_H + 1 + j - up) * RPB_C + WIN_C - GRID_W,
                                      [[1, GRID_W], [RPB_R * RPB_C, HEADS], [1, GRID_W]])
                        pool.dma_start(a_tb[64 * up:64 * up + 64, :, j, :], src)\
                            .then_inc(S(f"na{l}_rpb").handle, 16)
                low_to(AT["mla", l][0] + 2)
                end()
                low_to(AT["merge", l][0] + 2)
                mb = [k for _, _, k in merge_body(l, 0)]
                end()
                pool.dma_start(arena[:, 0:KC * TOK], x_spill).then_inc(S("restored").handle, 16)
                n0, body = AT["merge", l][0], 6
                with pool.Fori(0, 3) as i:
                    for j in range(body):
                        low(n0 + j + 2, mb[(j + 2) % body], BLK, i, body)
                done[0] = n0 + 3 * body + 2
                low_to(AT["ff", l][0] + 2)
                end()
                norm_low(l, 1, t0)
                n0, body = AT["ff", l][0], 8
                with pool.Fori(0, 3) as i:
                    for j in range(body):
                        low(n0 + j + 2, KC, BLK, i, body)
                done[0] = n0 + 3 * body + 2
                low_to(n0 + 4 * body)
                end()

        @block.scalar
        def _(act):
            steps = Steps(act, S("act_step").handle)
            link = steps.link
            phase = [0]

            def end():
                phase[0] += 1
                barrier(act, phase[0])

            def load(dst, src, name="par_in"):
                act.dma_start(dst, src).then_inc(S(name).up(16), 16)

            load(const[:, :], a["consts"], "const_in")
            act.wait_ge(*S("zeroed").at(1))
            for row, n, src in ((R_G1, 8, a["g_norm1"]), (R_G2, 8, a["g_norm2"]), (R_BMOD, 48, a["b_mod"]),
                                (R_GOUT, 4, a["ml_g_out"]), (R_GCQ, 3, a["mla_g_cq"]), (R_GCKV, 2, a["mla_g_ckv"])):
                load(prow[row:row + n, :, :], src.rearrange("l (r c) -> r l c", c=P))
            for row, src, w in ((R_GQ, a["mla_g_q"], MLA_D), (R_GK, a["mla_g_k"], MLA_D),
                                (R_NGQ, a["na_g_q"], NA_D), (R_NGK, a["na_g_k"], NA_D)):
                for c in range(0, P - w + 1, w):
                    load(prow[row:row + 1, :, c:c + w], src.rearrange("(a l) w -> a l w", a=1))
            load(prow[R_C:R_C + 8, 0, :], a["c"][0].rearrange("(r c) -> r c", c=P))
            load(prow[R_CC:R_CC + 8, 0, :], a["c_ctx"].rearrange("(r c) -> r c", c=P))
            for which, src in ((0, a["mla_g_q"]), (1, a["mla_g_k"])):
                load(ropeg[:, :, which, :], bass.AP(src.tensor, src.offset + NOPE, [[0, P], [MLA_D, DEPTH], [1, ROPE]]))
            for which, src in ((0, a["ml_i_bias"]), (1, a["ml_f_bias"])):
                for l in range(DEPTH):
                    for d in range(2):
                        load(bias4[:, l, which, d:d + 1], src[l, d].rearrange("(h a) -> h a", a=1))

            def high(n, k, w, u_used, i=None, body=0, body_u=0, first=False):
                act.wait_ge(*S(f"raw_full{n % 2}").at(16 * (half(n, i, body) + 1) if i is not None else 16 * (n // 2 + 1)))
                if w == 64:
                    act.wait_ge(*S("raw_gates").at(16 if n < AT["ml", 1][0] else 32))
                if type(u_used) is tuple:
                    act.wait_ge(*S("side_full").at(u_used[0] + 1))
                elif u_used is not None:
                    act.wait_ge(*S(f"bank_full{2 * (u_used % 2) + 1}").at(half(u_used, i, body_u) + 1))
                cut = cut_chunk(k) * w
                for part in (slice(0, cut), slice(cut, k * w)):
                    act.activation(wH[:, n % 2, part], raw[:, n % 2, part], ACT.Copy)\
                        .then_inc(S("w_high").handle, 1)

            def full(u, b, i=None, body=0):
                act.wait_ge(*S(f"bank_full{2 * (u % 2) + b}").at(half(u, i, body) + 1))
                return bank[2 * (u % 2) + b]

            def free(u, b):
                return S(f"bank_free{2 * (u % 2) + b}").handle

            table = {}
            for n in range(8):
                table[n] = (KC, BLK, (n,))
            for l in range(DEPTH):
                for name in ("ml", "na", "wout"):
                    n0, u0 = AT[name, l]
                    for j, (_, k, w) in enumerate(phase_blocks(name, l)):
                        table[n0 + j] = (k, w, u0 + j)
                        if name == "na" and j >= 6:
                            table[n0 + j] = (k, w, (SIDE_AT["na", l] + j - 6,))
                n0, u0 = AT["mla", l]
                for j, (_, k, w) in enumerate(phase_blocks("mla", l)):
                    if j < 6:
                        u0 += mla_units(l)[j]
                    table[n0 + j] = (k, w, u0 - 1 if j < 6 else (SIDE_AT["mla", l] + j - 6,))
                for name, make, body in loops(l):
                    n0, u0 = AT[name, l]
                    for j, (_, _, k) in enumerate(make(l, 0)):
                        for i in range(4):
                            table[n0 + i * body + j] = (k, BLK, u0 + i * body + j)

            def ahead(n):
                if n + 2 < N_BLOCKS:
                    k, w, _ = table[n + 2]
                    high(n + 2, k, w, table[n][2])

            def ahead_in_loop(n0, u0, j, body, i):
                k, w, _ = table[n0 + j + 2]
                high(n0 + j + 2, k, w, u0 + j, i, body, body)

            def exp_and_ln():
                act.preload_act_table_set("natural_log_exp_and_others")

            def square(l, which, t0, c):
                tag = f"nrm{l}{which}_"
                if c >= 2:
                    act.wait_ge(*S(tag + "sum").at(c - 1))
                act.activation(n_sq[:, c % 2, t0:TOK], x[:, c, t0:TOK], ACT.Square).then_inc(S(tag + "sq").up(1), 1)

            def norm(l, which, t0):
                tag = f"nrm{l}{which}_"
                exp_and_ln()
                if (l, which) != (0, 0):
                    for c in range(KC):
                        square(l, which, t0, c)
                act.wait_ge(*S(tag + "sum").at(KC))
                link(act.activation(n_std[:, t0:TOK], bank[4][:, t0:TOK], ACT.Ln, scale=1.0 / D, bias=eps[:, 0:1]))
                act.activation(n_std[:, t0:TOK], n_std[:, t0:TOK], ACT.Exp, scale=-0.5)\
                    .then_inc(S(tag + "std").up(1), 1)
                sh = M_SH1 if which == 0 else M_SH2
                for c in range(KC):
                    act.wait_ge(*S(tag + "t").at(c + 1))
                    for s, lo in ((CTXS, 0), (LAT, CTX)):
                        if lo >= t0:
                            act.activation(
                                hH[:, c, lo:lo + 256], n_t[:, c % 2, lo:lo + 256], ACT.Identity,
                                scale=gain[:, c, s:s + 1], bias=modT[:, l, sh + c, s:s + 1]).then_inc(S(tag + "high").up(1), 1)

            high(0, *table[0][:2], None)
            high(1, *table[1][:2], None)
            act.wait_ge(*S("par_T").at(DEPTH))
            cc = par[:, 0, R_C:R_C + 16].rearrange("p (s k) -> p s k", s=2)
            act.wait_ge(*S("zeroed").at(3))
            act.activation(csilu[:, :, :], cc, ACT.Sigmoid).then_inc(S("c_sig").up(1), 1)
            act.wait_ge(*S("c_silu").at(1))
            for s in range(2):
                act.activation(ccols[:, :, 2 * s], csilu[:, s, :], ACT.Copy).then_inc(S("c_high").up(1), 1)
            act.wait_ge(*S("xT_done").at(8))
            for n in range(8):
                ahead(n)
                square(0, 0, 0, n)
            for l in range(DEPTH):
                t0 = first_token(l)
                nt = TOK - t0
                norm(l, 0, 0)
                n0, u0 = AT["ml", l]
                act.wait_ge(*S("spilled").at(16 * (l + 1)))
                for j in range(7):
                    ahead(n0 + j)
                    for b in range(2):
                        if j == 1:
                            act.activation(m_k[:, b, :], full(u0 + j, b)[:, :], ACT.Copy).then_inc(free(u0 + j, b), 1)
                        if j in (4, 5):
                            act.activation(m_o[:, 2 * (j - 4) + b, t0:], full(u0 + j, b)[:, t0:TOK], ACT.Sigmoid)\
                                .then_inc(free(u0 + j, b), 1)
                tag = f"ml{l}_"
                for d in range(2):
                    act.wait_ge(*S(tag + "nz").at(d + 1))
                    link(act.activation(m_e[0:4, :], m_e[0:4, :], ACT.Exp))
                    act.activation(m_e[0:4, :], m_e[0:4, :], ACT.Ln, bias=1.0).then_inc(S(tag + "ln").up(1), 1)

                def decays(hd):
                    h, d = divmod(hd, 2)
                    for e_at, kt, lo, hi, diag in ml_pieces(d, t0):
                        e = m_E[d][:, e_at, 0:hi - lo]
                        n_arg[0] += 1
                        act.wait_ge(*S(tag + "arg").at(n_arg[0]))
                        act.activation(e, e, ACT.Exp, scale=-1.0).then_inc(S(tag + "exp").up(1), 1)

                n_arg = [0]
                exp_and_ln()
                decays(0)
                for it in range(2 * ML_H + 2):
                    if 1 <= it <= 2 * ML_H:
                        act.wait_ge(*S(tag + "dm").at(it))
                        link(act.activation(m_d[:, t0:], m_d[:, t0:], ACT.Ln))
                        act.activation(m_d[:, t0:], m_d[:, t0:], ACT.Exp, scale=-1.0).then_inc(S(tag + "rc").up(1), 1)
                    if it + 1 < 2 * ML_H:
                        decays(it + 1)
                    if it < 2 * ML_H:
                        act.wait_ge(*S(tag + "nm").at(it + 1))
                        if it > 0:
                            act.wait_ge(*S(tag + "dm").at(it))
                        act.activation(m_en[:, t0:], bank[0][:, t0:TOK], ACT.Exp).then_inc(S(tag + "en").up(1), 1)
                    h = it // 2 - 1
                    if h >= 0 and it % 2 == 0:
                        act.wait_ge(*S(tag + "ssum").at(h + 1))
                        link(act.activation(m_sq[:, t0:], bank[3][:, t0:TOK], ACT.Ln,
                                            scale=1.0 / ML_DV, bias=eps[:, 0:1]))
                        act.activation(m_sq[:, t0:], m_sq[:, t0:], ACT.Exp, scale=-0.5)\
                            .then_inc(S(tag + "std").up(1), 1)
                    if h >= 0 and it % 2 == 1:
                        act.wait_ge(*S(tag + "y").at(h + 1))
                        act.activation(oH[:, h, t0:], m_h[h % 2][:, t0:], ACT.Copy).then_inc(S(tag + "oH").up(1), 1)
                end()
                for br in ("na", "mla"):
                    tag = f"{br}{l}_"
                    n0, u0 = AT[br, l]
                    nb = list(norm_banks(br, l))
                    if br == "mla":
                        for j in range(3):
                            ahead(n0 + j)
                            if j < 2:
                                for b in range(2):
                                    c = 2 * j + b
                                    lo = t0 if c < 3 else 0
                                    act.activation(l_c[:, c, lo:], full(u0 + j, b)[:, lo:TOK], ACT.Copy)\
                                        .then_inc(free(u0 + j, b), 1)
                        for u, b in ((u0 + 1, 1), (u0 + 2, 1)):
                            act.wait_ge(*S(f"bank_free{2 * (u % 2) + b}").at(u // 2 + 1))
                        for c in range(5):
                            lo = t0 if c < 3 else 0
                            if c > 0:
                                act.wait_ge(*S(tag + "csum").at(c))
                            act.activation(s_sq[:, lo:], l_c[:, c, lo:], ACT.Square).then_inc(S(tag + "csq").up(1), 1)
                        act.wait_ge(*S(tag + "csum").at(5))
                        act.activation(st[:, 0, t0:], bank[4][:, t0:TOK], ACT.Ln, scale=1.0 / MLA_QR, bias=eps[:, 0:1])
                        link(act.activation(st[:, 1, :], bank[5][:, :], ACT.Ln, scale=1.0 / MLA_KVR, bias=eps[:, 0:1]))
                        act.activation(st[:, 0, t0:], st[:, 0, t0:], ACT.Exp, scale=-0.5)\
                            .then_inc(S(tag + "cstd").up(1), 1)
                        act.activation(st[:, 1, :], st[:, 1, :], ACT.Exp, scale=-0.5)\
                            .then_inc(S(tag + "cstd").up(1), 1)
                        for c in range(5):
                            lo = t0 if c < 3 else 0
                            act.wait_ge(*S(tag + "cn").at(c + 1))
                            act.activation(oH[:, 8 + c, lo:], l_c[:, c, lo:], ACT.Copy).then_inc(S(tag + "cH").up(1), 1)
                        for t in range(NTILE):
                            act.activation(l_t[:, 0:ROPE], small[:, t, 32:64], ACT.Square).then_inc(S(tag + "krs").up(1), 1)
                            act.wait_ge(*S(tag + "krsum").at(t + 1))
                    def queries_out(m):
                        is_q, t, ntl, h0, nh = nb[m]
                        if not is_q:
                            return
                        act.wait_ge(*S(tag + "tr").at(m + 1))
                        tb = bank[4 + m % 2]
                        if br == "na":
                            act.wait_ge(*S(tag + "zero").at(1))
                            for up in range(2):
                                r = slice(64 * up, 64 * up + 64)
                                for tt in range(ntl):
                                    src = tb[r, tt * 256:tt * 256 + 256].rearrange("p (a t) -> p a t", a=2)
                                    dst = a_q[r, h0 + up:h0 + 4:2, (t + tt) * P:(t + tt) * P + P]
                                    ins = act.activation(dst, src, ACT.Copy, scale=gcols[r, 0:1])
                            ins.then_inc(S(tag + "trq").up(1), 1)
                        else:
                            src = tb[0:MLA_D, :].rearrange("p (a t) -> p a t", a=4)
                            dst = l_q[0:MLA_D, h0:h0 + 4, t * P:t * P + P]
                            act.activation(dst, src, ACT.Copy, scale=gcols[0:MLA_D, 0:1]).then_inc(S(tag + "trq").up(1), 1)

                    def deviation(m):
                        _, _, ntl, _, nh = nb[m]
                        at = 64 * (m % 2)
                        act.wait_ge(*S(tag + "ss").at(m + 1))
                        rs = stat[:, at + 8:at + 8 + ntl * nh]
                        act.activation(rs, stat[:, at:at + ntl * nh], ACT.Sqrt,
                                            scale=1.0 / (NA_D if br == "na" else MLA_D), bias=eps[:, 0:1]).then_inc(S(tag + "nstd").up(1), 1)

                    act.wait_ge(*S(tag + "g").at(1))
                    for m, (is_q, t, ntl, h0, nh) in enumerate(nb):
                        G = ntl * nh
                        if br == "na":
                            u, b = u0 + m // 2, m % 2
                            W = pitch = NA_D
                            if b == 1:
                                ahead(n0 + m // 2)
                        else:
                            u, b = u0 + 3 + m // 2, m % 2
                            W = MLA_D if is_q else NOPE
                            pitch = MLA_D if is_q else 128
                            for jj in (3, 4, 5):
                                if b == 1 and table[n0 + jj][2] == u:
                                    ahead(n0 + jj)
                        src = full(u, b)[:, 0:G * pitch].rearrange("p (g w) -> p g w", w=pitch)[:, :, 0:W]
                        if m >= 2:
                            act.wait_ge(*S(tag + "ss").at(m - 1))
                        sq = (s_sq, s_sq2)[m % 2]
                        act.activation(sq[:, 0:G * W].rearrange("p (g w) -> p g w", w=W),
                                       src, ACT.Square).then_inc(S(tag + "nsq").up(1), 1)
                        if m:
                            deviation(m - 1)
                        if m >= 2:
                            queries_out(m - 2)
                    deviation(len(nb) - 1)
                    queries_out(len(nb) - 2)
                    queries_out(len(nb) - 1)
                    if br == "na":
                        for j in (4, 5):
                            ahead(n0 + j)
                            for b in range(2):
                                dst = a_v[:, 2 * b:2 * b + 2, (j - 4) * BLK:(j - 3) * BLK]
                                act.activation(dst, full(u0 + j, b)[:, :].rearrange("p (t w) -> p t w", t=2), ACT.Copy)\
                                    .then_inc(free(u0 + j, b), 1)
                    items = [(qi, t, h) for qi, t in enumerate(att_tiles(l)) for h in range(HEADS)]
                    for step in range(len(items) + 3):
                        if step < len(items):
                            qi, t, h = items[step]
                            nk = att_keys(t) * P
                            biased = br == "na" and t >= 2
                            src = s_p[:, step % 2, 0:nk] if biased else bank[4 + step % 2][:, 0:nk]
                            act.wait_ge(*S(tag + "max").at(step + 1))
                            if step - 1 > 0:
                                act.wait_ge(*S(tag + "pt").at(step - 1))
                            if step - 1 > 0:
                                act.wait_ge(*S(tag + "oev").at(step - 1))
                            act.activation(s_p[:, step % 2, 0:nk], src, ACT.Exp,
                                                           bias=stat[:, 16 + step % 2:17 + step % 2],
                                                           accum_out=stat[:, 20 + step % 2:21 + step % 2]).then_inc(S(tag + "p").up(1), 1)
                        if 0 <= step - 1 < len(items):
                            k = step - 1
                            nk = att_keys(items[k][1]) * P
                            act.wait_ge(*S(tag + "pt").at(k + 1))
                            if k - 1 > 0:
                                act.wait_ge(*S(tag + "o").at(k - 1))
                            act.activation(s_pt[:, k % 2, 0:nk], bank[6 + k % 2][:, 0:nk], ACT.Copy).then_inc(S(tag + "pts").up(1), 1)
                        if step >= 3 and (step - 3) % HEADS == HEADS - 1:
                            qi, t, _ = items[step - 3]
                            act.wait_ge(*S(tag + "ot").at(qi + 1))
                            ob = 4 if br == "na" else 8
                            act.activation(oH[:, ob:ob + 4, t * P:t * P + P],
                                                            bank[2][:, :].rearrange("p (a t) -> p a t", a=4), ACT.Copy).then_inc(S(tag + "oH").up(1), 1)
                        side = side_step(br, l, step - 1)
                        if side is not None:
                            ahead(n0 + 6 + side)
                    end()
                n0, u0 = AT["merge", l]
                body = 6
                kinds = [k for k, _, _ in merge_body(l, 0)]

                def merge_turn(n0, u0, i, last):
                    for j, kind in enumerate(kinds):
                        if last:
                            ahead(n0 + j)
                        else:
                            ahead_in_loop(n0, u0, j, body, i)
                        if kind == "gate":
                            for b in range(2):
                                act.wait_ge(*S(f"bank_free{2 * ((u0 + j - 1) % 2) + b}").at(half(u0 + j - 1, i, body) + 1))
                                act.activation(g_sig[:, b, t0:], full(u0 + j, b, i, body)[:, t0:TOK], ACT.Sigmoid)\
                                    .then_inc(free(u0 + j, b), 1)
                with act.Fori(0, 3) as i:
                    merge_turn(n0, u0, i, False)
                merge_turn(n0 + 3 * body, u0 + 3 * body, None, True)
                for c in range(KC):
                    act.wait_ge(*S(f"mg{l}_acc").at(1))
                    act.activation(hH[:, c, t0:], g_acc[:, c, t0:], ACT.Copy).then_inc(S(f"mg{l}_high").up(1), 1)
                n0, u0 = AT["wout", l]
                for j in range(4):
                    ahead(n0 + j)
                end()
                norm(l, 1, t0)
                n0, u0 = AT["ff", l]
                body = 8
                def turn(n0, u0, i, last):
                    def hidden(j, b):
                        c = 2 * j + b
                        if c >= 2:
                            act.wait_ge(*S(f"ff{l}_hid").at(count(c - 1, i, 8) if i is not None else 3 * 8 + c - 1))
                        bf = f"bank_free{2 * ((u0 + j) % 2) + b}"
                        act.activation(f_r[:, b, t0:], full(u0 + j, b, i, body)[:, t0:TOK], ACT.Relu)\
                            .then_inc(S(bf).handle, 1)
                        act.wait_ge(*S(bf).at(half(u0 + j, i, body) + 1))
                        act.activation(oH[:, c, t0:], f_r[:, b, t0:], ACT.Square)\
                            .then_inc(S(f"ff{l}_high").handle, 1)

                    for j in range(body):
                        for b in (0, 1) if j == 3 else (0,) if j < 3 else ():
                            hidden(j, b)
                        if not last:
                            ahead_in_loop(n0, u0, j, body, i)
                        else:
                            ahead(n0 + j)
                        if j < 3:
                            hidden(j, 1)
                last_peeled = l == DEPTH - 1
                with act.Fori(0, 4 - last_peeled) as i:
                    turn(n0, u0, i, False)
                if last_peeled:
                    turn(n0 + 3 * body, u0 + 3 * body, None, True)
                end()

        @block.vector
        def _(dve):
            steps = Steps(dve, S("dve_step").handle)
            link = steps.link
            phase = [0]

            def end():
                phase[0] += 1
                barrier(dve, phase[0])

            def full(u, b, i=None, body=0):
                dve.wait_ge(*S(f"bank_full{2 * (u % 2) + b}").at(half(u, i, body) + 1))
                return bank[2 * (u % 2) + b]

            def free(ins, u, b):
                ins.then_inc(S(f"bank_free{2 * (u % 2) + b}").handle, 1)

            def freed(u, b, i=None, body=0):
                dve.wait_ge(*S(f"bank_free{2 * (u % 2) + b}").at(half(u, i, body) + 1))

            def share(n, k, i=None, body=0):
                cut = cut_chunk(k) * BLK
                dve.wait_ge(*S("w_high").at(count(2 * n + 1, i, 2 * body)))
                dve.tensor_tensor(wL[:, n % 2, 0:cut], raw[:, n % 2, 0:cut],
                                  wH[:, n % 2, 0:cut].bitcast(F32), ALU.subtract)\
                    .then_inc(S("w_share").handle, 1 if i is not None else share_step(n))

            def share_ahead(n):
                if n + 2 < N_BLOCKS and SHARED[n + 2]:
                    share(n + 2, share_k[n + 2])

            share_k = {n: KC for n in range(N_BLOCKS)}
            for l in range(DEPTH):
                for n in range(1, 24, 2):
                    share_k[AT["merge", l][0] + n] = 4

            def mod_out(g):
                l, chunk = g // MOD_BLOCKS, 2 * (g % MOD_BLOCKS)
                dve.wait_ge(*S("side_full").at(g + 1))
                dve.transpose(modt[:, :], bank[3][0:32, 0:BLK]).then_inc(S("side_free").up(1), 1)
                dve.wait_ge(*S("side_free").at(g + 1))
                for q in range(4):
                    t4 = modt[:, :].rearrange("p (b w) -> p b w", b=2)[:, :, 32 * q:32 * q + 4]
                    t4 = t4.rearrange("p b (s e) -> p b s e", e=2)
                    ins = dve.tensor_tensor(modT[32 * q:32 * q + 32, l, chunk:chunk + 2, :],
                                            t4[:, :, :, 0], t4[:, :, :, 1], ALU.add)
                link(ins)

            def add_bias(l, lo, hi):
                for s in range(2):
                    link(dve.tensor_tensor(modT[:, l, lo:hi, s], modT[:, l, lo:hi, s],
                                           par[:, l, R_BMOD + lo:R_BMOD + hi], ALU.add))

            def norm(l, which, t0):
                tag = f"nrm{l}{which}_"
                sh, sc, g = (M_SH1, M_SC1, R_G1) if which == 0 else (M_SH2, M_SC2, R_G2)
                for s in range(2):
                    link(dve.scalar_tensor_tensor(gain[:, :, s], modT[:, l, sc:sc + KC, s], 1.0,
                                                  par[:, l, g:g + KC], ALU.add, ALU.mult))
                dve.wait_ge(*S(tag + "std").at(1))
                halves = [(s, lo) for s, lo in ((CTXS, 0), (LAT, CTX)) if lo >= t0]
                for c in range(KC):
                    if c >= 2:
                        dve.wait_ge(*S(tag + "high").at(len(halves) * (c - 1)))
                    dve.tensor_tensor(n_t[:, c % 2, t0:], x[:, c, t0:], n_std[:, t0:], ALU.mult)\
                        .then_inc(S(tag + "t").up(1), 1)
                    dve.wait_ge(*S(tag + "t").at(c + 1))
                    if c >= 2:
                        dve.wait_ge(*S(tag + "low").at(c - 1))
                    for s, lo in halves:
                        ins = dve.tensor_scalar(n_t2[:, c % 2, lo:lo + 256], n_t[:, c % 2, lo:lo + 256],
                                                gain[:, c, s:s + 1], modT[:, l, sh + c, s:s + 1], ALU.mult, ALU.add)
                    ins.then_inc(S(tag + "t2").up(1), 1)

            share(0, KC)
            share(1, KC)
            for l in range(DEPTH):
                dve.wait_ge(*S("par_rows").at(l + 1))
                dve.tensor_copy(par[:, l, :], bank[2 + l][:, 0:N_ROWS]).then_inc(S("par_T").up(1), 1)
            dve.wait_ge(*S("c_sig").at(1))
            cc = par[:, 0, R_C:R_C + 16].rearrange("p (s k) -> p s k", s=2)
            dve.tensor_tensor(csilu[:, :, :], csilu[:, :, :], cc, ALU.mult).then_inc(S("c_silu").up(1), 1)
            k = S("c_silu").n
            dve.wait_ge(*S("c_silu").at(k))
            dve.wait_ge(*S("c_high").at(2))
            for s in range(2):
                dve.tensor_tensor(ccols[:, :, 2 * s + 1], csilu[:, s, :],
                                                ccols[:, :, 2 * s].bitcast(F32), ALU.subtract).then_inc(S("c_low").up(1), 1)
            for c in range(KC):
                dve.wait_ge(*S("x_cols").at(c + 1))
                dve.tensor_copy(x[:, c, :], bank[4 + c % 4][:, :]).then_inc(S("xT_done").up(1), 1)
            for g in range(8):
                mod_out(g)
                share_ahead(g)
            add_bias(0, 0, 16)

            def rope(dst, src, at, tile, groups):
                cos = const[:, C_COS + ROPE * tile:C_COS + ROPE * (tile + 1)]
                sin = const[:, C_SIN + ROPE * tile:C_SIN + ROPE * (tile + 1)]
                t1, t2 = (at[:, k, 0:groups * ROPE].rearrange("p (g w) -> p g w", w=ROPE) for k in range(2))

                def over(v):
                    return v.rearrange("p (a w) -> p a w", a=1).broadcast_to([P, groups, v.shape[-1]])
                dve.tensor_tensor(t1, src, over(cos), ALU.mult)
                for part in range(2):
                    for hf in range(2):
                        o, w = part * 16 + hf * 8, part * 16 + (1 - hf) * 8
                        ins = dve.tensor_tensor(t2[:, :, o:o + 8], src[:, :, w:w + 8], over(sin[:, o:o + 8]), ALU.mult)
                link(ins)
                link(dve.tensor_tensor(dst, t1, t2, ALU.add))

            for l in range(DEPTH):
                t0 = first_token(l)
                norm(l, 0, 0)
                tag = f"ml{l}_"
                n0, u0 = AT["ml", l]
                dve.wait_ge(*S(tag + "zero").at(2))
                for b in range(2):
                    src = full(u0, b)
                    dve.tensor_scalar(m_qz[0:64, 2 * b, t0:], src[0:64, t0:TOK], ML_DK ** -0.5, None, ALU.mult)
                    free(dve.tensor_scalar(m_qz[64:128, 2 * b + 1, t0:], src[64:128, t0:TOK], ML_DK ** -0.5, None,
                                           ALU.mult), u0, b)
                for j in (2, 3):
                    for b in range(2):
                        free(dve.tensor_copy(m_v[:, 2 * b:2 * b + 2, (j - 2) * BLK:(j - 1) * BLK],
                                             full(u0 + j, b)[:, :].rearrange("p (t w) -> p t w", t=2)), u0 + j, b)
                narrow = m_tmp[0:64, :]
                free(dve.tensor_copy(narrow, full(u0 + 6, 0)[0:64, :]), u0 + 6, 0)
                freed(u0 + 6, 0)
                free(dve.tensor_tensor(narrow, narrow, full(u0 + 6, 1)[0:64, :], ALU.add), u0 + 6, 1)
                dve.wait_ge(*S(tag + "turned").at(1))
                dve.tensor_copy(small[:, :, :], bank[7][:, 0:256].rearrange("p (t w) -> p t w", t=NTILE))\
                    .then_inc(S(tag + "small").up(1), 1)
                for d in range(2):
                    ib, zb = bank[4 + 2 * d], bank[5 + 2 * d]
                    z, e, F, g = m_z[0:4, :], m_e[0:4, :], m_F[0:4, :], m_g[0:4, d, :]
                    dve.wait_ge(*S(tag + "rows").at(2 * d + 2))
                    link(dve.tensor_scalar(z, zb[0:4, :], bias4[:, l, 1, d:d + 1], None, ALU.add))
                    dve.scalar_tensor_tensor(e, z, -1.0, z, ALU.mult, ALU.min).then_inc(S(tag + "nz").up(1), 1)
                    dve.wait_ge(*S(tag + "ln").at(d + 1))
                    link(dve.scalar_tensor_tensor(z, z, 0.0, e, ALU.min, ALU.subtract))
                    M = m_rows[0:4, d, :]

                    def scan(out_, in_, op):
                        if d == 0:
                            link(dve.tensor_tensor_scan(out_, in_, in_, 0.0, op, ALU.bypass))
                        else:
                            c, r = slice(0, CTX), slice(CTX, TOK)
                            link(dve.tensor_tensor_scan(out_[:, c][:, ::-1], in_[:, c][:, ::-1], in_[:, c][:, ::-1],
                                                        0.0, op, ALU.bypass))
                            link(dve.tensor_tensor_scan(out_[:, r][:, ::-1], in_[:, r][:, ::-1], in_[:, r][:, ::-1],
                                                        out_[:, 0:1], op, ALU.bypass))
                    scan(F, z, ALU.add)
                    link(dve.scalar_tensor_tensor(g, ib[0:4, :], bias4[:, l, 0, d:d + 1], F, ALU.add, ALU.subtract))
                    scan(M, g, ALU.max)
                    dve.scalar_tensor_tensor(m_rows[0:4, 2 + d, :], F, -1.0, M,
                                                                     ALU.mult, ALU.subtract).then_inc(S(tag + "nmrow").up(1), 1)
                    k = S(tag + "nmrow").n
                    dve.wait_ge(*S(tag + "nmrow").at(k))
                dve.wait_ge(*S(tag + "gT").at(1))
                dve.tensor_copy(gcol, bank[3][:, 0:32]).then_inc(S(tag + "gcol").up(1), 1)
                k = S(tag + "gcol").n
                dve.wait_ge(*S(tag + "gcol").at(k))
                def arguments(hd):
                    h, d = divmod(hd, 2)
                    dve.wait_ge(*S(tag + "bcM").at(hd + 1))
                    if hd >= 2:
                        dve.wait_ge(*S(tag + "nd").at(hd - 1))
                    for e_at, kt, lo, hi, diag in ml_pieces(d, t0):
                        c = (d * 4 + kt) * 4 + h
                        dve.tensor_scalar(m_E[d][:, e_at, 0:hi - lo], bank[7][:, lo:hi], gcol[:, c:c + 1], 0.0,
                                          ALU.subtract, ALU.max).then_inc(S(tag + "arg").up(1), 1)

                nd_, k = 0, 0
                arguments(0)
                arguments(1)
                for it in range(2 * ML_H + 3):
                    h, d = divmod(it, 2)
                    if it < 2 * ML_H:
                        if d == 0:
                            dve.wait_ge(*S(tag + "sc").at(h + 1))
                        for e_at, kt, lo, hi, diag in ml_pieces(d, t0):
                            k += 1
                            dve.wait_ge(*S(tag + "exp").at(k))
                            if diag is not None:
                                nd_ += 1
                                dve.wait_ge(*S(tag + "mask").at(nd_))
                            sbk = bank[4 + kt // 2] if lo >= CTX else bank[6]
                            o = (kt % 2) * 256 + lo % CTX
                            if lo < CTX:
                                o = kt * 256 + lo
                            e = m_E[d][:, e_at, 0:hi - lo]
                            dve.tensor_tensor(e, e, sbk[:, o:o + hi - lo], ALU.mult).then_inc(S(tag + "P").up(1), 1)
                    if 1 <= it <= 2 * ML_H:
                        h, d = divmod(it - 1, 2)
                        dve.wait_ge(*S(tag + "nd").at(it))
                        dve.wait_ge(*S(tag + "en").at(it))
                        link(dve.tensor_tensor(m_d[:, t0:], bank[2][:, t0:TOK], m_en[:, t0:], ALU.max))
                        dve.scalar_tensor_tensor(m_d[:, t0:], bank[2][:, t0:TOK], -1.0, m_d[:, t0:],
                                                 ALU.mult, ALU.max).then_inc(S(tag + "dm").up(1), 1)
                        if it + 1 < 2 * ML_H:
                            arguments(it + 1)
                        dve.wait_ge(*S(tag + "rc").at(it))
                        dst = m_h[h % 2] if d == 0 else m_tmp
                        dve.tensor_tensor(dst[:, t0:], bank[1][:, t0:TOK], m_d[:, t0:], ALU.mult)\
                            .then_inc(S(tag + "acc").up(1), 1)
                        dve.wait_ge(*S(tag + "acc").at(it))
                        if d == 1:
                            mh = m_h[h % 2][:, t0:]
                            dve.tensor_tensor(mh, mh, m_tmp[:, t0:], ALU.add).then_inc(S(tag + "h").up(1), 1)
                            dve.wait_ge(*S(tag + "h").at(h + 1))
                            dve.tensor_tensor(m_sq[:, t0:], mh, mh, ALU.mult).then_inc(S(tag + "sq").up(1), 1)
                    h = (it - 3) // 2
                    if h >= 0 and it % 2 == 1:
                        mh = m_h[h % 2][:, t0:]
                        dve.wait_ge(*S(tag + "std").at(h + 1))
                        link(dve.tensor_tensor(mh, mh, m_sq[:, t0:], ALU.mult))
                        dve.scalar_tensor_tensor(mh, mh, par[:, l, R_GOUT + h:R_GOUT + h + 1],
                                                 m_o[:, h, t0:], ALU.mult, ALU.mult).then_inc(S(tag + "y").up(1), 1)
                        dve.wait_ge(*S(tag + "y").at(h + 1))
                    if h >= 0 and it % 2 == 0:
                        dve.wait_ge(*S(tag + "oH").at(h + 1))
                        link(dve.tensor_tensor(oL[:, h, t0:], m_h[h % 2][:, t0:], oH[:, h, t0:].bitcast(F32),
                                               ALU.subtract))
                end()
                for br in ("na", "mla"):
                    tag = f"{br}{l}_"
                    n0, u0 = AT[br, l]
                    nb = list(norm_banks(br, l))
                    if br == "na":
                        dve.tensor_scalar(gcols[:, 0:1], par[:, l, R_NGQ:R_NGQ + 1], NA_SCALE, None, ALU.mult)
                        dve.tensor_copy(gcols[:, 1:2], par[:, l, R_NGK:R_NGK + 1]).then_inc(S(tag + "g").up(1), 1)
                        kk = S(tag + "g").n
                        dve.wait_ge(*S(tag + "rpb").at(12 * 16))
                        mask = const[:, C_MASK:C_MASK + GRID_W].rearrange("p (a w) -> p a w", a=1)
                        tb = a_tb.rearrange("p h j w -> p (h j) w")
                        link(dve.tensor_tensor(tb, tb, mask.broadcast_to([P, 48, GRID_W]), ALU.add))
                    else:
                        dve.memset(gcols[:, 0:1], MLA_SCALE)
                        link(dve.memset(gcols[:, 1:2], 1.0))
                        dve.tensor_scalar(gcols[0:64, 0:1], par[0:64, l, R_GQ:R_GQ + 1], MLA_SCALE, None, ALU.mult)
                        dve.tensor_copy(gcols[0:64, 1:2], par[0:64, l, R_GK:R_GK + 1]).then_inc(S(tag + "g").up(1), 1)
                        kk = S(tag + "g").n
                        free(dve.tensor_copy(l_c[:, 4, :], full(u0 + 2, 0)[:, :]), u0 + 2, 0)
                        freed(u0 + 2, 0)
                        free(dve.tensor_tensor(l_c[:, 4, :], l_c[:, 4, :], full(u0 + 2, 1)[:, :], ALU.add), u0 + 2, 1)
                        freed(u0 + 2, 1)
                        dve.wait_ge(*S(tag + "cstd").at(2))
                        for c in range(5):
                            lo = t0 if c < 3 else 0
                            dve.scalar_tensor_tensor(l_c[:, c, lo:], l_c[:, c, lo:],
                                                                      par[:, l, R_GCQ + c:R_GCQ + c + 1],
                                                                      st[:, int(c >= 3), lo:], ALU.mult, ALU.mult).then_inc(S(tag + "cn").up(1), 1)
                        dve.wait_ge(*S(tag + "cn").at(5))
                        for c in range(5):
                            lo = t0 if c < 3 else 0
                            dve.wait_ge(*S(tag + "cH").at(c + 1))
                            dve.tensor_tensor(oL[:, 8 + c, lo:], l_c[:, c, lo:],
                                                               oH[:, 8 + c, lo:].bitcast(F32), ALU.subtract).then_inc(S(tag + "cL").up(1), 1)
                        dve.wait_ge(*S(tag + "cL").at(5))
                        for t in range(NTILE):
                            dve.wait_ge(*S(tag + "krs").at(t + 1))
                            dve.reduce_sum(stat[:, 32 + t:33 + t], l_t[:, 0:ROPE], axis=AX).then_inc(S(tag + "krsum").up(1), 1)
                            kr = l_kr[:, t:t + 1, :]
                            link(dve.tensor_tensor(kr, small[:, t:t + 1, 32:64], ropeg[:, l, 1:2, :], ALU.mult))
                            if t >= 2:
                                rope(kr, kr, l_r, t - 2, 1)
                    nq = sum(q for q, *_ in nb)

                    def keys_out(m):
                        is_q, t, ntl, h0, nh = nb[m]
                        if is_q:
                            return
                        dve.wait_ge(*S(tag + "tr").at(m + 1))
                        tb = bank[4 + m % 2]
                        if br == "na":
                            for tt in range(ntl):
                                src = tb[:, tt * 256:tt * 256 + 256].rearrange("p (a t) -> p a t", a=2)
                                ins = dve.tensor_scalar(a_k[:, h0 // 2:h0 // 2 + 2, (t + tt) * P:(t + tt) * P + P], src,
                                                        gcols[:, 1:2], None, ALU.mult)
                        else:
                            src = tb[0:MLA_D, :].rearrange("p (a t) -> p a t", a=4)
                            ins = dve.tensor_scalar(l_k[0:MLA_D, h0:h0 + 4, t * P:t * P + P], src,
                                                    gcols[0:MLA_D, 1:2], None, ALU.mult)
                        ins.then_inc(S(tag + "trk").up(1), 1)

                    dve.wait_ge(*S(tag + "g").at(kk))
                    def shape(m):
                        is_q, _, ntl, _, nh = nb[m]
                        if br == "na":
                            return ntl * nh, NA_D, NA_D, NA_D
                        return (nh, MLA_D, MLA_D, MLA_D) if is_q else (nh, NOPE, 128, MLA_D)

                    def sums(m):
                        G, W, _, _ = shape(m)
                        at = 64 * (m % 2)
                        dve.wait_ge(*S(tag + "nsq").at(m + 1))
                        if m >= 2:
                            dve.wait_ge(*S(tag + "nstd").at(m - 1))
                        red = dve.reduce_sum(stat[:, at:at + G], (s_sq, s_sq2)[m % 2][:, 0:G * W]
                                             .rearrange("p (g w) -> p g w", w=W), axis=AX)
                        if br == "mla" and not nb[m][0]:
                            link(red)
                            t = nb[m][1]
                            red = dve.tensor_scalar(stat[:, at:at + G], stat[:, at:at + G],
                                                    stat[:, 32 + t:33 + t], None, ALU.add)
                        red.then_inc(S(tag + "ss").up(1), 1)

                    def normalised(m):
                        is_q, t, ntl, h0, nh = nb[m]
                        G, W, pitch, wide = shape(m)
                        u, b = (u0 + m // 2, m % 2) if br == "na" else (u0 + 3 + m // 2, m % 2)
                        at = 64 * (m % 2)
                        dve.wait_ge(*S(tag + "nstd").at(m + 1))
                        link(dve.reciprocal(stat[:, at + 8:at + 8 + G], stat[:, at + 8:at + 8 + G]))
                        if m - 1 > 0:
                            dve.wait_ge(*S(tag + "tr").at(m - 1))
                        src = full(u, b)[:, 0:G * pitch].rearrange("p (g w) -> p g w", w=pitch)
                        dst = st[:, m % 2, 0:G * wide].rearrange("p (g w) -> p g w", w=wide)
                        rs = stat[:, at + 8:at + 8 + G].rearrange("p (g a) -> p g a", a=1)
                        if br == "mla" and not is_q:
                            dve.tensor_copy(l_v[:, t, h0 * 64:h0 * 64 + 256].rearrange("p (g w) -> p g w", w=64),
                                            src[:, :, NOPE:128])
                        free(dve.tensor_tensor(dst[:, :, 0:W], src[:, :, 0:W], rs.broadcast_to([P, G, W]), ALU.mult), u, b)
                        if br == "mla":
                            freed(u, b)
                            r = dst[:, :, NOPE:MLA_D]
                            if is_q:
                                link(dve.tensor_tensor(r, r, ropeg[:, l, 0:1, :].broadcast_to([P, G, ROPE]), ALU.mult))
                                if t >= 2:
                                    rope(r, r, l_r, t - 2, G)
                                dve.tensor_copy(stat[0:1, 60:61], stat[0:1, at + 8:at + 9]).then_inc(S(tag + "st").up(1), 1)
                            else:
                                dve.tensor_tensor(
                                    r, l_kr[:, t:t + 1, :].broadcast_to([P, G, ROPE]),
                                    rs.broadcast_to([P, G, ROPE]), ALU.mult).then_inc(S(tag + "st").up(1), 1)

                    for m in range(len(nb) + 1):
                        if m < len(nb):
                            sums(m)
                        if m:
                            normalised(m - 1)
                        if m >= 2:
                            keys_out(m - 2)
                    keys_out(len(nb) - 1)
                    items = [(qi, t, h) for qi, t in enumerate(att_tiles(l)) for h in range(HEADS)]
                    for step in range(len(items) + 3):
                        if step < len(items):
                            qi, t, h = items[step]
                            nk = att_keys(t) * P
                            s_bank = bank[4 + step % 2]
                            dve.wait_ge(*S(tag + "s").at(step + 1))
                            if step - 1 > 0:
                                dve.wait_ge(*S(tag + "p").at(step - 1))
                            if br == "na" and t >= 2:
                                if step - 1 > 0:
                                    dve.wait_ge(*S(tag + "pt").at(step - 1))
                                j0 = 2 if t == 2 else 0
                                dve.tensor_copy(s_p[:, step % 2, 0:CTX], s_bank[:, 0:CTX])
                                bias = a_tb[:, h, j0:j0 + 4, :].rearrange("p j w -> p (j w)")
                                link(dve.tensor_tensor(s_p[:, step % 2, CTX:TOK], s_bank[:, CTX:TOK], bias, ALU.add))
                                src = s_p[:, step % 2, 0:nk]
                            else:
                                src = s_bank[:, 0:nk]
                            dve.reduce_max(stat[:, 16 + step % 2:17 + step % 2], src, axis=AX,
                                                             negate=True).then_inc(S(tag + "max").up(1), 1)
                        if 0 <= step - 2 < len(items):
                            k = step - 2
                            qi, t, h = items[k]
                            dve.wait_ge(*S(tag + "o").at(k + 1))
                            link(dve.reciprocal(stat[:, 24 + k % 2:25 + k % 2], stat[:, 20 + k % 2:21 + k % 2]))
                            if qi - 1 > 0:
                                dve.wait_ge(*S(tag + "ot").at(qi - 1))
                            dve.tensor_scalar(s_o[:, qi % 2, h * 64:h * 64 + 64],
                                                                bank[k % 2][:, 64 * (h % 2):64 * (h % 2) + 64],
                                                                stat[:, 24 + k % 2:25 + k % 2], None, ALU.mult).then_inc(S(tag + "oev").up(1), 1)
                        if step >= 3 and (step - 3) % HEADS == HEADS - 1:
                            qi, t, _ = items[step - 3]
                            dve.wait_ge(*S(tag + "oH").at(qi + 1))
                            ob = 4 if br == "na" else 8
                            cols_ = slice(t * P, t * P + P)
                            dve.tensor_tensor(oL[:, ob:ob + 4, cols_],
                                                               bank[2][:, :].rearrange("p (a t) -> p a t", a=4),
                                                               oH[:, ob:ob + 4, cols_].bitcast(F32), ALU.subtract).then_inc(S(tag + "oL").up(1), 1)
                        side = side_step(br, l, step - 1)
                        if side is not None:
                            mod_out(SIDE_AT[br, l] + side)
                            share_ahead(n0 + 6 + side)
                    end()
                n0, u0 = AT["merge", l]
                body = 6

                def merge_turn(n0, u0, i, c0):
                    for j, (kind, _, _) in enumerate(merge_body(l, 0)):
                        if kind == "branch":
                            for b in range(2):
                                acc = g_acc[:, bass.ds(c0 + b, 1), t0:].rearrange("p a t -> p (a t)")
                                freed(u0 + j - 1, b, i, body)
                                src = full(u0 + j, b, i, body)[:, t0:TOK]
                                if j == 1:
                                    free(dve.tensor_tensor(acc, src, g_sig[:, b, t0:], ALU.mult), u0 + j, b)
                                else:
                                    free(dve.tensor_tensor(g_tmp[:, b, t0:], src, g_sig[:, b, t0:], ALU.mult), u0 + j, b)
                                    freed(u0 + j, b, i, body)
                                    link(dve.tensor_tensor(acc, acc, g_tmp[:, b, t0:], ALU.add))
                        if i is None:
                            share_ahead(n0 + j)
                        else:
                            share(n0 + j + 2, share_k[n0 + j + 2], i, body)
                with dve.Fori(0, 3) as i:
                    steps.enter(i, 4)
                    merge_turn(n0, u0, i, i * 2)
                    steps.leave(3)
                merge_turn(n0 + 3 * body, u0 + 3 * body, None, 6)
                dve.drain().then_inc(S(f"mg{l}_acc").handle, 1)
                if l == 0:
                    add_bias(0, 16, 48)
                    add_bias(1, 0, 32)
                else:
                    add_bias(1, 32, 48)
                for c in range(KC):
                    dve.wait_ge(*S(f"mg{l}_high").at(c + 1))
                    dve.tensor_tensor(hL[:, c, t0:], g_acc[:, c, t0:],
                                                         hH[:, c, t0:].bitcast(F32), ALU.subtract).then_inc(S(f"mg{l}_low").up(1), 1)

                def residual(u, c, gate, i=None, body=0):
                    for b in range(2):
                        src = full(u, b, i, body)
                        for s, lo in ((CTXS, 0), (LAT, CTX)):
                            if lo < t0:
                                continue
                            ins = dve.scalar_tensor_tensor(x[:, c + b, lo:lo + 256], src[:, lo:lo + 256],
                                                           modT[:, l, gate + c + b, s:s + 1], x[:, c + b, lo:lo + 256],
                                                           ALU.mult, ALU.add)
                        free(ins, u, b)

                dve.wait_ge(*S("restored").at(16 * (l + 1)))
                n0, u0 = AT["wout", l]
                for j in range(4):
                    residual(u0 + j, 2 * j, M_GATE1)
                    share_ahead(n0 + j)
                end()
                norm(l, 1, t0)
                n0, u0 = AT["ff", l]
                body = 8

                def ff_turn(n0, u0, i, done8):
                    def hidden_low(j, b):
                        c = 2 * j + b
                        freed(u0 + j, b, i, body)
                        link(dve.tensor_tensor(f_h[:, b, t0:], f_r[:, b, t0:], f_r[:, b, t0:], ALU.mult))
                        dve.wait_ge(*S(f"ff{l}_high").at(done8 + c + 1))
                        dve.tensor_tensor(oL[:, c, t0:], f_h[:, b, t0:], oH[:, c, t0:].bitcast(F32),
                                          ALU.subtract).then_inc(S(f"ff{l}_hid").handle, 1)
                        if c == 7:
                            dve.wait_ge(*S(f"ff{l}_hid").at(done8 + 8))

                    for j in range(8):
                        for b in (0, 1) if j == 3 else (0,) if j < 3 else ():
                            hidden_low(j, b)
                        if j >= 4:
                            residual(u0 + j, 2 * (j - 4), M_GATE2, i, body)
                        if i is None:
                            share_ahead(n0 + j)
                        else:
                            share(n0 + j + 2, KC, i, body)
                        if j < 3:
                            hidden_low(j, 1)
                with dve.Fori(0, 3) as i:
                    steps.enter(i, 8)
                    ff_turn(n0, u0, i, i * 8)
                    steps.leave(3)
                ff_turn(n0 + 3 * body, u0 + 3 * body, None, 24)
                end()
            for k in range(4):
                dve.wait_ge(*S("y_rows").at(k + 1))
                dve.tensor_copy(xtok[:, 2 + k // 2, (k % 2) * 512:(k % 2) * 512 + 512], bank[4 + k][:, :]).then_inc(S("y_tok").up(1), 1)

        @block.tensor
        def _(pe):
            phase = [0]

            def end():
                phase[0] += 1
                barrier(pe, phase[0])

            def begin(u, b, i=None, body=0):
                if i is not None or u >= 2:
                    pe.wait_ge(*S(f"bank_free{2 * (u % 2) + b}").at(half(u, i, body)))
                return bank[2 * (u % 2) + b]

            def filled(ins, u, b):
                ins.then_inc(S(f"bank_full{2 * (u % 2) + b}").handle, 1)

            def weights(n, k, w, i=None, body=0, first_chunks=False):
                if SHARED[n]:
                    pe.wait_ge(*S("w_share").at(count(n + 1, i, body)))
                if not (SHARED[n] and first_chunks):
                    pe.wait_ge(*S("w_split").at(count(n + 1, i, body)))
                return slot(wH, n, k, w), slot(wL, n, k, w)

            def features(n, u, k, cuts, rH, rL, i=None, body=0, ready=None):
                H, L = weights(n, k, BLK if cuts[0][0] != cuts[1][0] else P, i, body, first_chunks=True)
                for b, (c, k0, kn, lo) in enumerate(cuts):
                    dst = begin(u, b, i, body)[:, lo:TOK]
                    for kk in range(k0, k0 + kn):
                        if SHARED[n] and b == 0 and kk == cut_chunk(k):
                            pe.wait_ge(*S("w_split").at(count(n + 1, i, body)))
                        if ready is not None and b == 0:
                            pe.wait_ge(*ready(kk))
                        for m, (w_, r_) in enumerate(((H, rH), (H, rL), (L, rH))):
                            ins = pe.matmul(dst, w_[:, kk, c:c + P], r_[:, kk, lo:TOK],
                                            start=kk == k0 and m == 0, stop=kk == k0 + kn - 1 and m == 2)
                    filled(ins, u, b)

            def both(k, lo):
                return [(0, 0, k, lo), (P, 0, k, lo)]

            def tokens(n, u, k, w, parts, sH, sL):
                H, L = weights(n, k, w)
                for b, part in enumerate(parts):
                    bk = begin(u, b)
                    for t, at, c, width in part:
                        for kk in range(k):
                            for m, (s_, w_) in enumerate(((sH, H), (sH, L), (sL, H))):
                                ins = pe.matmul(bk[:, at:at + width], s_[:, kk, t * P:t * P + P],
                                                w_[:, kk, c:c + width],
                                                start=kk == 0 and m == 0, stop=kk == k - 1 and m == 2)
                    filled(ins, u, b)

            def modulation(n, g):
                H, L = weights(n, KC, BLK)
                if g:
                    pe.wait_ge(*S("side_free").at(g))
                for kk in range(KC):
                    for m, w_ in enumerate((H, L)):
                        ins = pe.matmul(bank[3][:, 0:BLK], ccols[:, kk, :], w_[:, kk, :],
                                        start=kk == 0 and m == 0, stop=kk == KC - 1 and m == 1)
                ins.then_inc(S("side_full").up(1), 1)

            def drained(u_next):
                for u in (u_next - 2, u_next - 1):
                    for b in range(2):
                        pe.wait_ge(*S(f"bank_free{2 * (u % 2) + b}").at(u // 2 + 1))

            def norm(l, which, t0):
                for c in range(KC):
                    square_sum(l, which, t0, c)

            def square_sum(l, which, t0, c):
                tag = f"nrm{l}{which}_"
                pe.wait_ge(*S(tag + "sq").at(c + 1))
                pe.matmul(bank[4][:, t0:TOK], ones, n_sq[:, c % 2, t0:TOK],
                          start=c == 0, stop=c == KC - 1).then_inc(S(tag + "sum").up(1), 1)

            pe.wait_ge(*S("const_in").at(16))
            pe.wait_ge(*S("par_in").at(S("par_in").n))
            for l in range(DEPTH):
                pe.transpose(bank[2 + l][:, 0:N_ROWS], prow[:, l, :], ident[0:N_ROWS, 0:N_ROWS]).then_inc(S("par_rows").up(1), 1)
            pe.wait_ge(*S("x_in").at(32))
            for c in range(KC):
                if c - 3 > 0:
                    pe.wait_ge(*S("xT_done").at(c - 3))
                for t in range(NTILE):
                    ins = pe.transpose(bank[4 + c % 4][:, t * P:t * P + P], xtok[:, t, c * P:c * P + P], ident)
                ins.then_inc(S("x_cols").up(1), 1)
            pe.wait_ge(*S("c_low").at(2))
            pe.wait_ge(*S("par_T").at(2))
            pe.wait_ge(*S("xT_done").at(8))
            for g in range(8):
                modulation(g, g)
                square_sum(0, 0, 0, g)
            for l in range(DEPTH):
                t0 = first_token(l)
                if l:
                    norm(l, 0, 0)
                tag = f"ml{l}_"
                n0, u0 = AT["ml", l]
                two = [[(2 * b + s, 256 * s, 0, BLK) for s in range(2)] for b in range(2)]
                features(n0, u0, KC, both(KC, t0), hH, hL, ready=lambda kk: S(f"nrm{l}0_low").at(kk + 1))
                features(n0 + 1, u0 + 1, KC, both(KC, 0), hH, hL)
                tokens(n0 + 2, u0 + 2, KC, BLK, two, hH, hL)
                tokens(n0 + 3, u0 + 3, KC, BLK, two, hH, hL)
                features(n0 + 4, u0 + 4, KC, both(KC, t0), hH, hL)
                features(n0 + 5, u0 + 5, KC, both(KC, t0), hH, hL)
                H, L = weights(n0 + 6, KC, 64)
                for b in range(2):
                    dst = begin(u0 + 6, b)[0:64, :]
                    for kk in range(4 * b, 4 * b + 4):
                        for m, (w_, r_) in enumerate(((H, hH), (H, hL), (L, hH))):
                            ins = pe.matmul(dst, w_[:, kk, :], r_[:, kk, :],
                                            start=kk == 4 * b and m == 0, stop=kk == 4 * b + 3 and m == 2)
                    filled(ins, u0 + 6, b)
                drained(u0 + 7)
                for t in range(NTILE):
                    ins = pe.transpose(bank[7][:, t * 64:t * 64 + 64], m_tmp[0:64, t * P:t * P + P], ident[0:64, 0:64])
                ins.then_inc(S(tag + "turned").up(1), 1)
                pe.wait_ge(*S(tag + "small").at(1))
                for r in range(4):
                    for t in range(NTILE):
                        ins = pe.transpose(bank[4 + r][0:4, t * P:t * P + P], small[:, t, 4 * r:4 * r + 4], ident)
                    ins.then_inc(S(tag + "rows").up(1), 1)
                for d in range(2):
                    pe.wait_ge(*S(tag + "nmrow").at(d + 1))
                    for t in range(NTILE):
                        at = (d * 4 + t) * 4
                        ins = pe.transpose(bank[3][:, at:at + 4], m_g[0:4, d, t * P:t * P + P], ident[0:4, 0:4])
                ins.then_inc(S(tag + "gT").up(1), 1)
                pieces = len(ml_pieces(0, t0))
                pe.wait_ge(*S(tag + "gcol").at(1))

                def broadcast_max(hd):
                    h, d = divmod(hd, 2)
                    if hd:
                        pe.wait_ge(*S(tag + "arg").at(pieces * hd))
                    pe.matmul(bank[7][:, t0:TOK], const[:, C_SEL + P * h:C_SEL + P * h + P], m_rows[:, d, t0:TOK],
                              start=True, stop=True).then_inc(S(tag + "bcM").up(1), 1)

                def scores(h):
                    for kt in range(4):
                        ins = pe.matmul(bank[4 + kt // 2][:, kt % 2 * 256:kt % 2 * 256 + 256],
                                        m_k[:, h // 2, kt * P:kt * P + P], m_qz[:, h, CTX:TOK], start=True, stop=True)
                    if t0 == 0:
                        for kt in range(2):
                            ins = pe.matmul(bank[6][:, kt * 256:kt * 256 + 256], m_k[:, h // 2, kt * P:kt * P + P],
                                            m_qz[:, h, 0:CTX], start=True, stop=True)
                    ins.then_inc(S(tag + "sc").up(1), 1)

                def square_sums(h):
                    pe.wait_ge(*S(tag + "sq").at(h + 1))
                    pe.matmul(bank[3][:, t0:TOK], ones, m_sq[:, t0:TOK], start=True, stop=True)\
                        .then_inc(S(tag + "ssum").up(1), 1)

                broadcast_max(0)
                scores(0)
                for it in range(2 * ML_H):
                    h, d = divmod(it, 2)
                    if it > 0:
                        pe.wait_ge(*S(tag + "en").at(it))
                    pe.matmul(bank[0][:, t0:TOK], const[:, C_SEL + P * h:C_SEL + P * h + P],
                              m_rows[:, 2 + d, t0:TOK], start=True, stop=True).then_inc(S(tag + "nm").up(1), 1)
                    if it + 1 < 2 * ML_H:
                        broadcast_max(it + 1)
                    pe.wait_ge(*S(tag + "P").at(pieces * (it + 1)))
                    if d == 1 and h + 1 < ML_H:
                        scores(h + 1)
                    if d == 0 and h > 0:
                        square_sums(h - 1)
                    if it > 0:
                        pe.wait_ge(*S(tag + "acc").at(it))
                    for lo_, hi_ in ((CTX, TOK), (0, CTX)):
                        group = [p for p in ml_pieces(d, t0) if lo_ <= p[2] < hi_]
                        for q, (e_at, kt, lo, hi, _) in enumerate(group):
                            for bk, lhs in ((1, m_v[:, kt, h * ML_DV:h * ML_DV + ML_DV]), (2, ones)):
                                ins = pe.matmul(bank[bk][:, lo:hi], lhs, m_E[d][:, e_at, 0:hi - lo],
                                                start=q == 0, stop=q == len(group) - 1)
                    ins.then_inc(S(tag + "nd").up(1), 1)
                square_sums(ML_H - 1)
                end()
                for br in ("na", "mla"):
                    tag = f"{br}{l}_"
                    n0, u0 = AT[br, l]
                    nb = list(norm_banks(br, l))
                    nq = sum(q for q, *_ in nb)
                    if br == "mla":
                        features(n0, u0, KC, both(KC, t0), hH, hL)
                        features(n0 + 1, u0 + 1, KC, [(0, 0, KC, t0), (P, 0, KC, 0)], hH, hL)
                        features(n0 + 2, u0 + 2, KC, [(0, 0, 4, 0), (0, 4, 4, 0)], hH, hL)
                        for c in range(5):
                            lo = t0 if c < 3 else 0
                            pe.wait_ge(*S(tag + "csq").at(c + 1))
                            pe.matmul(bank[4 if c < 3 else 5][:, lo:TOK], ones, s_sq[:, lo:TOK],
                                                         start=c in (0, 3), stop=c in (2, 4)).then_inc(S(tag + "csum").up(1), 1)
                        pe.wait_ge(*S(tag + "cL").at(5))

                    def unit(k):
                        if br == "na":
                            one = [[(2 + b, 0, 0, BLK)] for b in range(2)]
                            tokens(n0 + k, u0 + k, KC, BLK, one if (l == 1 and k < 2) else two, hH, hL)
                        elif k < nq // 2:
                            per = nq // 4
                            parts = [[(nb[2 * k + b][1], 0, 0, 384)] for b in range(2)]
                            tokens(n0 + 3 + k // per, u0 + 3 + k, 3, 384, parts, oH[:, 8:13], oL[:, 8:13])
                        else:
                            t = k - nq // 2
                            parts = [[(t, 0, 512 * b, 512)] for b in range(2)]
                            tokens(n0 + 5, u0 + 3 + k, 2, 1024, parts, oH[:, 11:13], oL[:, 11:13])

                    def turn_round(m):
                        is_q, t, ntl, h0, nh = nb[m]
                        if br == "na":
                            u, b = u0 + m // 2, m % 2
                            pe.wait_ge(*S(f"bank_free{2 * (u % 2) + b}").at(u // 2 + 1))
                        else:
                            pe.wait_ge(*S(tag + "st").at(m + 1))
                        if m >= 2:
                            if m - 2 < nq:
                                if m - 1 > 0:
                                    pe.wait_ge(*S(tag + "trq").at(m - 1))
                            else:
                                if m - 1 - nq > 0:
                                    pe.wait_ge(*S(tag + "trk").at(m - 1 - nq))
                        dst = bank[4 + m % 2]
                        n, w = (2 * ntl, P) if br == "na" else (4, MLA_D)
                        for q in range(n):
                            ins = pe.transpose(dst[0:w, q * P:q * P + P], st[:, m % 2, q * w:q * w + w],
                                               flip if br == "na" and is_q else ident)
                        ins.then_inc(S(tag + "tr").up(1), 1)
                    for k in range(len(nb) // 2):
                        unit(k)
                        if k:
                            turn_round(2 * k - 2)
                            turn_round(2 * k - 1)
                    if br == "na":
                        for k in (len(nb) // 2, len(nb) // 2 + 1):
                            unit(k)
                            if k == len(nb) // 2:
                                turn_round(2 * k - 2)
                                turn_round(2 * k - 1)
                        drained(u0 + 6)
                    else:
                        turn_round(len(nb) - 2)
                        turn_round(len(nb) - 1)
                        drained(u0 + 3 + len(nb) // 2)
                    pe.wait_ge(*S(tag + "trq").at(nq))
                    if len(nb) - nq > 0:
                        pe.wait_ge(*S(tag + "trk").at(len(nb) - nq))
                    items = [(qi, t, h) for qi, t in enumerate(att_tiles(l)) for h in range(HEADS)]
                    for step in range(len(items) + 3):
                        if step < len(items):
                            qi, t, h = items[step]
                            nk = att_keys(t) * P
                            if br == "na":
                                q_, k_ = a_q[:, h, t * P:t * P + P], a_k[:, h // 2, 0:nk]
                            else:
                                q_, k_ = l_q[0:MLA_D, h, t * P:t * P + P], l_k[0:MLA_D, h, 0:nk]
                            if step - 1 > 0:
                                pe.wait_ge(*S(tag + "p").at(step - 1))
                            pe.matmul(bank[4 + step % 2][:, 0:nk], q_, k_, start=True, stop=True).then_inc(S(tag + "s").up(1), 1)
                        if 0 <= step - 1 < len(items):
                            k = step - 1
                            pe.wait_ge(*S(tag + "p").at(k + 1))
                            if k - 1 > 0:
                                pe.wait_ge(*S(tag + "pts").at(k - 1))
                            for c in range(att_keys(items[k][1])):
                                ins = pe.transpose(bank[6 + k % 2][:, c * P:c * P + P], s_p[:, k % 2, c * P:c * P + P], ident)
                            ins.then_inc(S(tag + "pt").up(1), 1)
                        if 0 <= step - 2 < len(items):
                            k = step - 2
                            qi, t, h = items[k]
                            v_ = a_v if br == "na" else l_v
                            pe.wait_ge(*S(tag + "pts").at(k + 1))
                            if k - 1 > 0:
                                pe.wait_ge(*S(tag + "oev").at(k - 1))
                            nt_ = att_keys(t)
                            for c in range(nt_):
                                ins = pe.matmul(bank[k % 2][:, 0:P], s_pt[:, k % 2, c * P:c * P + P],
                                                v_[:, c, (h // 2) * P:(h // 2) * P + P], start=c == 0, stop=c == nt_ - 1)
                            ins.then_inc(S(tag + "o").up(1), 1)
                        if step >= 3 and (step - 3) % HEADS == HEADS - 1:
                            qi, t, _ = items[step - 3]
                            pe.wait_ge(*S(tag + "oev").at(HEADS * (qi + 1)))
                            if qi > 0:
                                pe.wait_ge(*S(tag + "oL").at(qi))
                            for c in range(4):
                                ins = pe.transpose(bank[2][:, c * P:c * P + P], s_o[:, qi % 2, c * P:c * P + P],
                                                   flip if br == "na" else ident)
                            ins.then_inc(S(tag + "ot").up(1), 1)
                        side = side_step(br, l, step)
                        if side is not None:
                            modulation(n0 + 6 + side, SIDE_AT[br, l] + side)
                    end()
                n0, u0 = AT["merge", l]
                body = 6
                with pe.Fori(0, 4) as i:
                    for j, (kind, _, k) in enumerate(merge_body(l, 0)):
                        if kind == "gate":
                            features(n0 + j, u0 + j, KC, both(KC, t0), hH, hL, i, body)
                        else:
                            br = j // 2
                            o = (0, 8, 4)[br]
                            features(n0 + j, u0 + j, 4, both(4, t0), oH[:, o:o + 4], oL[:, o:o + 4], i, body)
                n0, u0 = AT["wout", l]
                for j in range(4):
                    features(n0 + j, u0 + j, KC, both(KC, t0), hH, hL,
                             ready=(lambda kk: S(f"mg{l}_low").at(kk + 1)) if j == 0 else None)
                end()
                norm(l, 1, t0)
                n0, u0 = AT["ff", l]
                body = 8
                with pe.Fori(0, 4) as i:
                    for j, (kind, _, k) in enumerate(ff_body(l, 0)):
                        if kind == "up":
                            features(n0 + j, u0 + j, KC, both(KC, t0), hH, hL, i, body,
                                     (lambda kk: S(f"nrm{l}1_low").at(kk + 1)) if j == 0 else None)
                        else:
                            features(n0 + j, u0 + j, KC, both(KC, t0), oH, oL, i, body,
                                     (lambda kk: S(f"ff{l}_hid").at(i * 8 + (kk + 1))) if j == 4 else None)
                end()
            for k in range(4):
                for c in range(4):
                    cc = (k % 2) * 4 + c
                    lo = CTX + (k // 2) * P
                    ins = pe.transpose(bank[4 + k][:, c * P:c * P + P], x[:, cc, lo:lo + P], ident)
                ins.then_inc(S("y_rows").up(1), 1)
        for name, s in sems.items():
            phase, _, what = name.partition("_")
            kind = phase.rstrip("0123456789")
            if kind in ("ml", "na", "mla", "nrm") and phase != kind:
                turn = 2 * int(phase[3]) + int(phase[4]) if kind == "nrm" else int(phase[-1])
                assert s.n in (0, signals(kind, turn)[what]), (name, s.n)


INPUTS = ["x", "c", "ctx", "c_ctx", "w_mod", "b_mod", "g_norm1", "g_norm2", "w_in", "ml_i_bias", "ml_f_bias",
          "ml_g_out", "ml_w_o", "mla_g_cq", "mla_w_uq", "mla_g_ckv", "mla_w_ukv", "mla_g_q", "mla_g_k", "mla_w_o",
          "na_g_q", "na_g_k", "na_rpb", "na_w_o", "w_out", "w_ff1", "w_ff2"]


def kernel(**inputs):
    import concourse.bacc as bacc
    from concourse.bass_utils import run_bass_kernel_spmd

    nc = bacc.Bacc("TRN2", target_bir_lowering=False, num_devices=1)
    arrays = {name: np.ascontiguousarray(inputs[name]) for name in INPUTS}
    arrays["consts"] = shape_constants()
    aps = {name: nc.dram_tensor(f"in_{name}", v.shape, mybir.dt.from_np(v.dtype), kind="ExternalInput").ap()
           for name, v in arrays.items()}
    out = nc.dram_tensor("y", (1, SEQ, D), F32, kind="ExternalOutput").ap()
    build(nc, aps, out)
    r = run_bass_kernel_spmd(nc, [{f"in_{name}": v for name, v in arrays.items()}], core_ids=[0])
    return r.results[0]["y"]
```
